# Optimizing a Trainium2 kernel written in Bass

```python
import math
import jax
import jax.numpy as jnp
from jax import lax
import numpy as np

D_MODEL = 1024
BATCH = 1
SEQ = 512
DEPTH = 1
DEC_BATCH = 1
DEC_SEQ = 32
PAST_LEN = 128

CHUNK = 64
N_HEADS = D_MODEL // 128
HEAD_DIM = 64
V_DIM = 2 * HEAD_DIM
QK_WIDTH = N_HEADS * 2 * HEAD_DIM
V_WIDTH = N_HEADS * V_DIM
ROT_DIM = HEAD_DIM // 4
ROPE_THETA = 500000.0
ATTN_SCALE = HEAD_DIM ** -0.5
Q_BLOCK = 128
POOL_WINDOWS = (2, 4, 8, 16)
N_POOL_GROUPS = 4
POOL_WIDTH = D_MODEL // 2
POOL_GROUP_DIM = POOL_WIDTH // N_POOL_GROUPS
POOL_BUF = max(POOL_WINDOWS) - 1
N_EXPERT_GROUPS = 4
EXPERTS_PER_GROUP = 4
N_EXPERTS = N_EXPERT_GROUPS * EXPERTS_PER_GROUP
EXPERT_TOP_K = 2
EXPERT_HIDDEN = D_MODEL // 2
IN_WIDTH = POOL_WIDTH + 2 * QK_WIDTH + V_WIDTH + 2 * D_MODEL
IN_SPLITS = (POOL_WIDTH, POOL_WIDTH + QK_WIDTH, POOL_WIDTH + 2 * QK_WIDTH, POOL_WIDTH + 2 * QK_WIDTH + V_WIDTH)
RMS_EPS = 1e-6

kernel_name = 'hybrid_pool_diffattn_hiermoe_stream_step'

def rms_norm(x, g):
    xf = x.astype(jnp.float32)
    xf = xf * lax.rsqrt(jnp.mean(xf * xf, axis=-1, keepdims=True) + RMS_EPS)
    return xf.astype(x.dtype) * g

def rope_partial(x, pos):
    inv_freq = jnp.power(ROPE_THETA, -jnp.arange(0, ROT_DIM, 2, dtype=jnp.float32) / ROT_DIM)
    ang = pos.astype(jnp.float32)[:, None] * inv_freq[None, :]
    cos = jnp.cos(ang)[:, None, None, :]
    sin = jnp.sin(ang)[:, None, None, :]
    xr = x[..., :ROT_DIM].astype(jnp.float32)
    x1, x2 = xr[..., :ROT_DIM // 2], xr[..., ROT_DIM // 2:]
    rot = jnp.concatenate([x1 * cos - x2 * sin, x2 * cos + x1 * sin], axis=-1).astype(x.dtype)
    return jnp.concatenate([rot, x[..., ROT_DIM:]], axis=-1)

def pool_mixer(u, buf, pos, pool_w, pool_scale):
    B, T, _ = u.shape
    ext = jnp.concatenate([buf, u], axis=1)
    cs = jnp.cumsum(ext.astype(jnp.float32), axis=1)
    cs = jnp.concatenate([jnp.zeros_like(cs[:, :1]), cs], axis=1)
    end = cs[:, POOL_BUF + 1:]
    uf = u.astype(jnp.float32)
    outs = []
    for g, w in enumerate(POOL_WINDOWS):
        sl = slice(g * POOL_GROUP_DIM, (g + 1) * POOL_GROUP_DIM)
        window_sum = end[..., sl] - cs[:, POOL_BUF + 1 - w:POOL_BUF + 1 - w + T, sl]
        count = jnp.minimum(w, pos + 1).astype(jnp.float32)[None, :, None]
        outs.append(window_sum / count - uf[..., sl])
    d = jnp.stack(outs, axis=2).astype(u.dtype)
    y = jnp.einsum('btgc,gce->btge', d, pool_w).reshape(B, T, POOL_WIDTH) * pool_scale
    return y, ext[:, -POOL_BUF:]

def diff_attend(q, k, v, mask, lam):
    s = jnp.einsum('bqhmd,bkhmd->bhmqk', q, k).astype(jnp.float32) * ATTN_SCALE
    s = jnp.where(mask, s, -jnp.inf)
    p = jax.nn.softmax(s, axis=-1)
    a = p[:, :, 0] - lam * p[:, :, 1]
    return jnp.einsum('bhqk,bkhv->bqhv', a.astype(v.dtype), v)

def diff_attn_prompt(q, k, v, lam):
    B, T = q.shape[0], q.shape[1]
    nb = T // Q_BLOCK
    q_blocks = jnp.moveaxis(q.reshape(B, nb, Q_BLOCK, N_HEADS, 2, HEAD_DIM), 1, 0)
    k_chunk = jnp.arange(T) // CHUNK

    def block(args):
        q_blk, start = args
        q_chunk = (start + jnp.arange(Q_BLOCK)) // CHUNK
        mask = k_chunk[None, :] <= q_chunk[:, None]
        return diff_attend(q_blk, k, v, mask, lam)

    out = lax.map(block, (q_blocks, jnp.arange(nb) * Q_BLOCK))
    return jnp.moveaxis(out, 0, 1).reshape(B, T, N_HEADS, V_DIM)

def hier_moe(h, w_router_group, b_router_group, w_router_expert, b_router_expert,
             w_expert_gate, w_expert_up, w_expert_down):
    B, T, _ = h.shape
    t = h.reshape(B * T, D_MODEL)
    g_logits = (t @ w_router_group).astype(jnp.float32) + b_router_group
    g_prob = jax.nn.softmax(g_logits, axis=-1)
    g_sel = jnp.argmax(g_logits, axis=-1)
    g_w = jnp.take_along_axis(g_prob, g_sel[:, None], axis=-1)
    e_logits_all = jnp.einsum('nd,gde->nge', t, w_router_expert).astype(jnp.float32) + b_router_expert
    e_logits = jnp.take_along_axis(e_logits_all, g_sel[:, None, None], axis=1)[:, 0]
    top_v, top_i = lax.top_k(e_logits, EXPERT_TOP_K)
    top_w = jax.nn.softmax(top_v, axis=-1) * g_w
    expert_id = g_sel[:, None] * EXPERTS_PER_GROUP + top_i
    combine = jnp.sum(jax.nn.one_hot(expert_id, N_EXPERTS, dtype=jnp.float32) * top_w[..., None], axis=1)
    y = jnp.zeros((B * T, D_MODEL), jnp.float32)
    for e in range(N_EXPERTS):
        hid = jax.nn.silu(t @ w_expert_gate[e]) * (t @ w_expert_up[e])
        y = y + combine[:, e:e + 1] * (hid @ w_expert_down[e]).astype(jnp.float32)
    return y.astype(h.dtype).reshape(B, T, D_MODEL)

def hybrid_layer(x, pos, pool_buf, k_past, v_past, lam_init,
                 norm_mix_g, w_in, b_gate, lambda_q1, lambda_k1, lambda_q2, lambda_k2, subln_g,
                 pool_w, pool_scale, w_pool_branch, w_attn_branch, w_out, norm_ffn_g,
                 w_router_group, b_router_group, w_router_expert, b_router_expert,
                 w_expert_gate, w_expert_up, w_expert_down):
    B, T, _ = x.shape
    h = rms_norm(x, norm_mix_g)
    z = h @ w_in
    u_pool, q, k, v, gate_logits = jnp.split(z, IN_SPLITS, axis=-1)
    q = rope_partial(q.reshape(B, T, N_HEADS, 2, HEAD_DIM), pos)
    k = rope_partial(k.reshape(B, T, N_HEADS, 2, HEAD_DIM), pos)
    v = v.reshape(B, T, N_HEADS, V_DIM)

    if pool_buf is None:
        pool_buf = jnp.zeros((B, POOL_BUF, POOL_WIDTH), u_pool.dtype)
    pool_y, new_pool = pool_mixer(u_pool, pool_buf, pos, pool_w, pool_scale)

    lam = (jnp.exp(jnp.sum(lambda_q1.astype(jnp.float32) * lambda_k1.astype(jnp.float32)))
           - jnp.exp(jnp.sum(lambda_q2.astype(jnp.float32) * lambda_k2.astype(jnp.float32))) + lam_init)
    if k_past is None:
        attn = diff_attn_prompt(q, k, v, lam)
    else:
        n_past = k_past.shape[1]
        k_all = jnp.concatenate([k_past.reshape(B, n_past, N_HEADS, 2, HEAD_DIM), k], axis=1)
        v_all = jnp.concatenate([v_past, v], axis=1)
        k_pos = jnp.concatenate([jnp.arange(n_past), pos])
        mask = (k_pos // CHUNK)[None, :] <= (pos // CHUNK)[:, None]
        attn = diff_attend(q, k_all, v_all, mask, lam)
    attn = (rms_norm(attn, subln_g) * (1.0 - lam_init)).reshape(B, T, V_WIDTH)

    g_pool = jax.nn.sigmoid(gate_logits[..., :D_MODEL] + b_gate[:D_MODEL])
    g_attn = jax.nn.sigmoid(gate_logits[..., D_MODEL:] + b_gate[D_MODEL:])
    merged = g_pool * (pool_y @ w_pool_branch) + g_attn * (attn @ w_attn_branch)
    x = x + merged @ w_out

    x = x + hier_moe(rms_norm(x, norm_ffn_g), w_router_group, b_router_group, w_router_expert,
                     b_router_expert, w_expert_gate, w_expert_up, w_expert_down)
    return x, k.reshape(B, T, N_HEADS, 2 * HEAD_DIM), v, new_pool

def setup_inputs(seed: int = 0) -> dict:
    key = jax.random.key(seed)
    ks = jax.random.split(key, 32)

    def nrm(k, shape, scale):
        return jax.random.normal(k, shape, jnp.float32) * scale

    def gain(k, shape):
        return 1.0 + 0.05 * jax.random.normal(k, shape, jnp.float32)

    L = DEPTH
    return {
        'x_prompt': nrm(ks[0], (BATCH, SEQ, D_MODEL), 1.0),
        'x_sample': nrm(ks[1], (DEC_BATCH, DEC_SEQ, D_MODEL), 1.0),
        'cache_k': nrm(ks[2], (L, DEC_BATCH, PAST_LEN, N_HEADS, 2 * HEAD_DIM), 1.0),
        'cache_v': nrm(ks[3], (L, DEC_BATCH, PAST_LEN, N_HEADS, V_DIM), 1.0),
        'state_pool': nrm(ks[4], (L, DEC_BATCH, POOL_BUF, POOL_WIDTH), 1.0),
        'norm_mix_g': gain(ks[5], (L, D_MODEL)),
        'w_in': nrm(ks[6], (L, D_MODEL, IN_WIDTH), D_MODEL ** -0.5),
        'b_gate': nrm(ks[7], (L, 2 * D_MODEL), 0.1),
        'lambda_q1': nrm(ks[8], (L, HEAD_DIM), 0.1),
        'lambda_k1': nrm(ks[9], (L, HEAD_DIM), 0.1),
        'lambda_q2': nrm(ks[10], (L, HEAD_DIM), 0.1),
        'lambda_k2': nrm(ks[11], (L, HEAD_DIM), 0.1),
        'subln_g': gain(ks[12], (L, V_DIM)),
        'pool_w': nrm(ks[13], (L, N_POOL_GROUPS, POOL_GROUP_DIM, POOL_GROUP_DIM), POOL_GROUP_DIM ** -0.5),
        'pool_scale': gain(ks[14], (L, POOL_WIDTH)),
        'w_pool_branch': nrm(ks[15], (L, POOL_WIDTH, D_MODEL), POOL_WIDTH ** -0.5),
        'w_attn_branch': nrm(ks[16], (L, V_WIDTH, D_MODEL), V_WIDTH ** -0.5),
        'w_out': nrm(ks[17], (L, D_MODEL, D_MODEL), D_MODEL ** -0.5),
        'norm_ffn_g': gain(ks[18], (L, D_MODEL)),
        'w_router_group': nrm(ks[19], (L, D_MODEL, N_EXPERT_GROUPS), D_MODEL ** -0.5),
        'b_router_group': nrm(ks[20], (L, N_EXPERT_GROUPS), 0.01),
        'w_router_expert': nrm(ks[21], (L, N_EXPERT_GROUPS, D_MODEL, EXPERTS_PER_GROUP), D_MODEL ** -0.5),
        'b_router_expert': nrm(ks[22], (L, N_EXPERT_GROUPS, EXPERTS_PER_GROUP), 0.01),
        'w_expert_gate': nrm(ks[23], (L, N_EXPERTS, D_MODEL, EXPERT_HIDDEN), D_MODEL ** -0.5),
        'w_expert_up': nrm(ks[24], (L, N_EXPERTS, D_MODEL, EXPERT_HIDDEN), D_MODEL ** -0.5),
        'w_expert_down': nrm(ks[25], (L, N_EXPERTS, EXPERT_HIDDEN, D_MODEL), EXPERT_HIDDEN ** -0.5),
        'final_norm_g': gain(ks[26], (D_MODEL,)),
    }

def reference(x_prompt, x_sample, cache_k, cache_v, state_pool,
              norm_mix_g, w_in, b_gate, lambda_q1, lambda_k1, lambda_q2, lambda_k2, subln_g,
              pool_w, pool_scale, w_pool_branch, w_attn_branch, w_out, norm_ffn_g,
              w_router_group, b_router_group, w_router_expert, b_router_expert,
              w_expert_gate, w_expert_up, w_expert_down, final_norm_g):
    pos_prompt = jnp.arange(x_prompt.shape[1])
    pos_sample = cache_k.shape[2] + jnp.arange(x_sample.shape[1])
    xp, xs = x_prompt, x_sample
    k_p, v_p, pool_p, k_s, v_s, pool_s = [], [], [], [], [], []
    for l in range(DEPTH):
        lam_init = 0.8 - 0.6 * math.exp(-0.3 * l)
        lp = (norm_mix_g[l], w_in[l], b_gate[l], lambda_q1[l], lambda_k1[l], lambda_q2[l], lambda_k2[l],
              subln_g[l], pool_w[l], pool_scale[l], w_pool_branch[l], w_attn_branch[l], w_out[l],
              norm_ffn_g[l], w_router_group[l], b_router_group[l], w_router_expert[l], b_router_expert[l],
              w_expert_gate[l], w_expert_up[l], w_expert_down[l])
        xp, kp, vp, pp = hybrid_layer(xp, pos_prompt, None, None, None, lam_init, *lp)
        xs, kss, vss, pss = hybrid_layer(xs, pos_sample, state_pool[l], cache_k[l], cache_v[l], lam_init, *lp)
        k_p.append(kp); v_p.append(vp); pool_p.append(pp)
        k_s.append(kss); v_s.append(vss); pool_s.append(pss)
    y_prompt = rms_norm(xp, final_norm_g)
    y_sample = rms_norm(xs, final_norm_g)
    new_k_prompt = jnp.stack(k_p)
    new_v_prompt = jnp.stack(v_p)
    new_pool_prompt = jnp.stack(pool_p)
    new_k_sample = jnp.stack(k_s)
    new_v_sample = jnp.stack(v_s)
    new_pool_sample = jnp.stack(pool_s)
    return (y_prompt, y_sample, new_k_prompt, new_v_prompt, new_pool_prompt, new_k_sample, new_v_sample, new_pool_sample)


_drawn_inputs = setup_inputs


def setup_inputs(seed=0):
    import zlib

    import numpy as np

    out = dict(_drawn_inputs(seed))
    spreads = {}
    factors = {'lambda_q2': 200.0,
     'b_router_group': 14.886,
     'b_router_expert': 7.612,
     'lambda_q1': 18.001,
     'lambda_k1': 64.0,
     'subln_g': 2.667,
     'pool_scale': 3.122}
    for name, (base, spread) in spreads.items():
        noise = np.random.default_rng([zlib.crc32(name.encode()), seed]).standard_normal(out[name].shape)
        drawn = base * np.exp(spread * noise) if base else spread * noise
        out[name] = jnp.asarray(drawn.astype(out[name].dtype))
    for name, factor in factors.items():
        out[name] = (out[name] * factor).astype(out[name].dtype)
    return out
```

```python
import math
from contextlib import ExitStack

import concourse.bass as bass
import numpy as np
from concourse import mybir

F32 = mybir.dt.float32
F32R = mybir.dt.float32r
I32 = mybir.dt.int32
ALU = mybir.AluOpType
ACT = mybir.ActivationFunctionType
AX = mybir.AxisListType

P = 128
D = 1024
KD = D // P
SEQ, DEC, PAST = 512, 32, 128
TOK = SEQ + DEC
HALF = TOK // 2
NT = 5
LAST = P - DEC
HEADS, HD, CHUNK = 8, 64, 64
POOLW, NG, GD, BUF = 512, 4, 128, 15
WINDOWS = (2, 4, 8, 16)
EPS = 1e-6
SCALE = HD ** -0.5
LAM_INIT = 0.8 - 0.6 * math.exp(-0.3 * 0)
ROT, THETA = 16, 500000.0
EXPERTS, EG, EPG, HID = 16, 4, 4, 512
Q0, GATE0 = POOLW, POOLW + 3 * D
NEG = -1e30
CLAMP, BIG_SCALE, BIG_SUM = 1.5e18, 2.0 ** -70, 2.0 ** 116
TILES_PER_EXPERT = -(-TOK // P)
ROWS = TILES_PER_EXPERT * EXPERTS
UW = BUF + SEQ + BUF + DEC
US = BUF + SEQ + BUF
SLOT = 1024
RA, S, RM = 4, 4, 24

C_ID, C_COS, C_SIN, C_INV, C_TRI, C_ONE = 0, 128, 288, 448, 508, 636
C_NEGH, C_NEGA, C_TOK, C_IOTA, C_VAL, C_BASE, C_TRASH, C_W = 764, 892, 1020, 1025, 1041, 1046, 1062, 1072


def constants():
    c = np.zeros((P, C_W), np.float32)
    c[:, C_ID:C_ID + P] = np.eye(P)
    pos = np.arange(NT * P).reshape(NT, P)
    pos[4] = np.concatenate([np.arange(SEQ - LAST, SEQ), PAST + np.arange(DEC)])
    inv = np.power(np.float32(THETA), -np.arange(0, ROT, 2, dtype=np.float32) / np.float32(ROT)).astype(np.float32)
    ang = (pos.astype(np.float32)[..., None] * inv).astype(np.float32)
    for col, f in ((C_COS, np.cos), (C_SIN, np.sin)):
        t = np.broadcast_to(f(ang)[:, :, None, :], (NT, P, 4, ROT // 2)).transpose(1, 0, 2, 3)
        c[:, col:col + 160] = t.reshape(P, 160)
    for g, w in enumerate(WINDOWS):
        c[:, C_INV + BUF * g:C_INV + BUF * (g + 1)] = 1.0 / np.minimum(w, np.arange(BUF) + 1)
    c[:, C_TRI:C_TRI + P] = np.triu(np.ones((P, P)), 1)
    c[:, C_ONE:C_ONE + P] = 1.0
    c[:, C_NEGH:C_NEGH + CHUNK] = NEG
    c[:, C_NEGA:C_NEGA + P] = NEG
    tok = np.arange(NT * P).reshape(NT, P).T.astype(np.float32)
    tok[:, 4] = np.arange(SEQ - LAST, TOK)
    c[:, C_TOK:C_TOK + NT] = tok
    c[:, C_IOTA:C_IOTA + EXPERTS] = np.arange(EXPERTS) - 99
    valid = np.ones((P, NT))
    valid[:LAST, 4] = 0
    c[:, C_VAL:C_VAL + NT] = valid
    for k in range(2):
        c[:LAST, C_TRASH + 8 + k] = ROWS * P + P * k + np.arange(LAST)
    c[:, C_BASE:C_BASE + EXPERTS] = np.arange(EXPERTS) * P
    return c


def build(nc, a, o):
    base0 = nc.sbuf_base
    base0 = (base0 + 63) // 64 * 64
    K = 1024
    ends = [0]

    def at(name, off, shape, dt=F32):
        n = int(np.prod(shape[1:])) * 4
        ends[0] = max(ends[0], off + n)
        return nc.alloc_sbuf_tensor_at(name, shape, dt, offset=base0 + off)

    def region(off):
        pos = [off]

        def take(name, shape, dt=F32):
            t = at(name, pos[0], shape, dt)
            pos[0] += (int(np.prod(shape[1:])) * 4 + 31) // 32 * 32
            return t
        take.pos = pos
        return take

    with ExitStack() as ctx:
        sem = lambda n: ctx.enter_context(nc.semaphore(n))

        wh = at("wh", 0, [P, S, SLOT], F32R)
        wl = at("wl", 16 * K, [P, S, SLOT], F32R)
        x = at("x", 32 * K, [P, NT, D])
        small = region(52 * K)
        cst = small("cst", [P, C_W])
        bg = small("bg", [P, 16])
        psc = small("psc", [P, NG])
        sbg = small("sbg", [P, 1])
        lamv = small("lamv", [P, 4, HD])
        lame = small("lame", [P, 2])
        nlam = small("nlam", [P, 1])
        ssx = small("ssx", [P, NT])
        rsx = small("rsx", [P, NT])
        mx = small("mx", [P, 2, 2])
        nb = small("nb", [P, 2, 2])
        esum = small("esum", [P, 2, 2])
        rinv = small("rinv", [P, 2, 2])
        ssa = small("ssa", [P, NT, HEADS])
        rsa = small("rsa", [P, NT, HEADS])
        ssb = small("ssb", [P, NT, HEADS])
        isb = small("isb", [P, NT, HEADS])
        fin = small("fin", [P, NT, HEADS])
        wgt = small("wgt", [P, NT, 2])
        yidx = small("yidx", [P, NT, 2], I32)
        tix = small("tix", [P, NT, 2], I32)
        idi = small("idi", [P, ROWS + 2], I32)
        wr = small("wr", [P, KD, EG + EXPERTS])
        rb = small("rb", [P, EG + EXPERTS])
        idn = small("idn", [P, 2], I32)
        cnt = small("cnt", [P, EXPERTS])
        over = small("over", [P, 1], I32)
        assert small.pos[0] <= 60 * K, small.pos[0]
        hr = region(60 * K)
        qkv = hr("qkv", [P, NT, 384])
        E = hr("E", [P, 2, 2, 512])
        Am = hr("Am", [P, 512])
        qkh = hr("qkh", [P, 2, TOK], F32R)
        qkl = hr("qkl", [P, 2, TOK], F32R)
        ckh = hr("ckh", [P, P], F32R)
        ckl = hr("ckl", [P, P], F32R)
        vh = hr("vh", [P, NT + 1, P], F32R)
        vl = hr("vl", [P, NT + 1, P], F32R)
        ckv = hr("ckv", [P, 2, P])
        ath = hr("ath", [P, 4, P], F32R)
        atl = hr("atl", [P, 4, P], F32R)
        assert hr.pos[0] <= 99 * K, hr.pos[0]
        r0 = region(60 * K)
        sq = r0("sq", [P, 2, D])
        xn = r0("xn", [P, 2, D])
        r1 = region(60 * K)
        dd = r1("dd", [P, NG, TOK])
        ddh = r1("ddh", [P, NG, TOK], F32R)
        ddl = r1("ddl", [P, NG, TOK], F32R)
        B1 = r1("B1", [P, NG, UW])
        sg = r1("sg", [P, 2, TOK])
        r2 = region(60 * K)
        mh = r2("mh", [P, KD, TOK], F32R)
        ml = r2("ml", [P, KD, TOK], F32R)
        gt = r2("gt", [P, 2, TOK])
        assert r2.pos[0] <= 99 * K
        r3 = region(60 * K)
        xg = r3("xg", [P, 2, D])
        xh = r3("xh", [P, KD, P], F32R)
        xl = r3("xl", [P, KD, P], F32R)
        hid = r3("hid", [P, HID])
        hsl = r3("hsl", [P, HID])
        hh = r3("hh", [P, 4, P], F32R)
        hl = r3("hl", [P, 4, P], F32R)
        yb = r3("yb", [P, 2, D])
        assert r3.pos[0] <= 99 * K
        att = at("att", 99 * K, [P, NT, HEADS, P])
        r4 = region(99 * K)
        plh = r4("plh", [P, NG, TOK], F32R)
        pll = r4("pll", [P, NG, TOK], F32R)
        hTh = at("hTh", 119 * K, [P, KD, TOK], F32R)
        hTl = at("hTl", 136 * K, [P, KD, TOK], F32R)
        mA = at("mA", 153 * K, [P, KD, TOK])
        U = at("U", 153 * K, [P, NG, UW])
        B2 = at("B2", 162 * K, [P, NG - 1, UW])
        gB = at("gB", 170 * K, [P, KD, TOK])
        rawA = at("rawA", 187 * K, [P, RA, SLOT])
        rawM = at("rawM", 99 * K, [P, RM, SLOT])
        r5 = region(195 * K)
        h2T = r5("h2T", [P, KD, P])
        lg = r5("lg", [P, NT, EG + EXPERTS])
        lsm = r5("lsm", [ROWS, P])
        ra = [r5(f"ra{i}", [P, NT, EXPERTS]) for i in range(6)]
        rt = r5("rt", [P, 16, NT])
        assert r5.pos[0] <= 203 * K, r5.pos[0]
        fy = at("fy", 119 * K, [P, 2, 2, D])
        ob = at("ob", 135 * K, [P, 2, D])
        fsq = at("fsq", 143 * K, [P, D])
        gb = at("gb", 203 * K, [P, D])
        rot = at("rot", 203 * K, [P, 4, 160])
        asq = at("asq", 203 * K + 2560, [P, 2, P])
        bsq = at("bsq", 203 * K + 3584, [P, P])
        stt = at("stt", 116 * K, [16, POOLW])
        zero = at("zero", 118 * K + 256, [P, P])
        pst = at("pst", 203 * K, [P, 2, POOLW])
        assert ends[0] + base0 <= nc.sbuf_usable_end, (ends[0], base0, nc.sbuf_usable_end)

        ps = ctx.enter_context(nc.psum_tensor("ps", [P, 8, 512], F32))

        h2d = nc.dram_tensor("h2_rows", [TOK, D], F32, kind="Internal").ap()
        lst = nc.dram_tensor("token_list", [ROWS * P + 2 * P, 1], F32, kind="Internal").ap()
        yd = nc.dram_tensor("expert_rows", [ROWS * P, D], F32, kind="Internal").ap()

        cst_in, w_small, x_in = sem("cst_in"), sem("w_small"), [sem(f"x_in{t}") for t in range(NT)]
        raw_in = [sem(f"raw_in{i}") for i in range(RA)]
        raw_h = [sem(f"raw_head{i}") for i in range(RA)]
        hi_done, lo_done, mm_done = sem("hi_done"), sem("lo_done"), sem("mm_done")
        dch, ach = sem("dve_chain"), sem("act_chain")
        ms_done, rt_done, xn_done, xt_mm, xt_hi, xt_lo = (sem(n) for n in (
            "ms_done", "root_done", "xn_done", "xt_mm", "xt_hi", "xt_lo"))
        st_in, st_mm, st_ev, pad_done = sem("state_in"), sem("state_mm"), sem("state_ev"), sem("pad_done")
        last_mm, ws_act, ws_dve, pool_done, dh_done, dl_done = (sem(n) for n in (
            "last_mm", "ws_act", "ws_dve", "pool_done", "pool_hi", "pool_lo"))
        out_done, lam_s, lam_e, lam_done = sem("out_done"), sem("lam_sums"), sem("lam_exp"), sem("lam_done")
        acc_mm, acc_ev, rope_done, vhi_done, vlo_done, ckv_in, kv_out = (sem(n) for n in (
            "acc_mm", "acc_ev", "rope_done", "vhi_done", "vlo_done", "ckv_in", "kv_out"))
        tr_mm, tr_hi, tr_lo, sc_mm, nb_done, exp_done, am_done, ta_mm, ath_done, atl_done, av_mm, av_ev = (
            sem(n) for n in ("tr_mm", "tr_hi", "tr_lo", "sc_mm", "nb_done", "exp_done", "am_done", "ta_mm",
                             "ath_done", "atl_done", "av_mm", "av_ev"))
        an_done, at_mm, at_hi, at_lo = sem("an_done"), sem("at_mm"), sem("at_hi"), sem("at_lo")
        ab_sum, ab_hi, ab_lo, o_mm, o_ev = (sem(n) for n in (
            "ab_sum", "ab_hi", "ab_lo", "o_mm", "o_ev"))
        gb_in, h2_done, h2_mm, h2_ev, lg_mm, gd_done, ge_done, sel_done, pos_mm, ix_done, sc_in, ls_in, ls_mm, id_done = (
            sem(n) for n in ("gain_in", "h2_done", "h2_mm", "h2_ev", "lg_mm", "gd_done", "ge_done",
                             "sel_done", "pos_mm", "ix_done", "list_out", "list_in", "list_mm", "id_done"))
        z_done, z_out = sem("zero_done"), sem("zero_out")
        sp_go = sem("sp_go")
        m_raw = [sem(f"m_raw{i}") for i in range(RM)]
        m_hi, m_lo, m_mm, p_ch, p_go, xg_mm, xg_hi, xg_lo = (sem(n) for n in (
            "m_hi", "m_lo", "m_mm", "pool_chain", "pool_go", "xg_mm", "xg_hi", "xg_lo"))
        si_done, hid_done, hid_mm, hid_hi, hid_lo, y_ev = (sem(n) for n in (
            "silu_done", "hid_done", "hid_mm", "hid_hi", "hid_lo", "y_ev"))
        g_in = [sem(f"gather_in{i}") for i in range(2)]
        y_out = [sem(f"y_out{i}") for i in range(2)]
        Y0 = (3 * 16, 2 * 16)
        fy_in = [sem(f"fy_in{i}") for i in range(2)]
        f_out = [sem(f"f_out{i}") for i in range(2)]
        f_ms, f_rt, f_done = (sem(n) for n in ("f_ms", "f_root", "f_done"))

        id_m = cst[:, C_ID:C_ID + P]
        col = lambda t: slice(P * t, P * t + P) if t < 4 else slice(TOK - P, TOK)
        w_in = a["w_in"][0]

        def columns(w, c0, rows0, rows=4):
            return w[rows0 * P:(rows0 + rows) * P, c0:c0 + 256].rearrange("(k p) n -> p k n", p=P)

        ws, jobs = [], []

        def job(stage, i, views):
            jobs.append((stage, i, list(range(len(ws), len(ws) + len(views)))))
            ws.extend(views)
        for i in range(2):
            job("u", i, [columns(w_in, 256 * i, 4 * q) for q in range(2)])
        for i in range(4):
            job("gB", i, [columns(w_in, GATE0 + D + 256 * i, 4 * q) for q in range(2)])
        jobs.append(("last", 0, []))
        job("pl", 0, [a["pool_w"][0].rearrange("g c e -> c g e")])
        jobs.append(("pl", 1, [len(ws) - 1]))
        for i in range(4):
            job("gA", i, [columns(w_in, GATE0 + 256 * i, 4 * q) for q in range(2)])
            job("pA", i, [columns(a["w_pool_branch"][0], 256 * i, 0)])
        H0 = len(ws)
        AB0 = H0 + 4 * HEADS
        O0 = AB0 + 8
        NCH = O0 + 8
        act_jobs = [j for j, (s, _, _) in enumerate(jobs) if s != "pA"]
        dve_jobs = [j for j, (s, _, _) in enumerate(jobs) if s in ("pl", "pA")]
        count = lambda js, j: sum(1 for v in js if v <= j)
        WH = 768

        def words(n):
            if n < H0:
                return 512 if n == jobs[7][2][0] else SLOT
            return WH if n < AB0 else SLOT

        def later_source(n):
            if n < O0:
                m, q = divmod(n - AB0, 2)
                return columns(a["w_attn_branch"][0], 256 * m, 4 * q)
            m, q = divmod(n - O0, 4)
            return a["w_out"][0][2 * P * q:2 * P * (q + 1), 512 * m:512 * (m + 1)].rearrange("(k p) n -> p k n", p=P)

        def head_source(h, k):
            return w_in[P * k:P * (k + 1), Q0:Q0 + 3 * D].rearrange(
                "p (s h c) -> p s h c", s=3, h=HEADS)[:, :, h, :]

        def arrival(n):
            return raw_in[n % RA], 16 * sum(1 for m in range(n + 1) if m % RA == n % RA and not H0 <= m < AB0)

        def raw_view(n, src):
            d = rawA[:, n % RA, 0:words(n)]
            return d.rearrange("p (k n) -> p k n", k=src.shape[1])

        new_k, new_v = o["new_k_prompt"][0, 0], o["new_v_prompt"][0, 0]
        new_ks, new_vs = o["new_k_sample"][0, 0], o["new_v_sample"][0, 0]
        moe_src = (a["w_expert_gate"][0], a["w_expert_up"][0], a["w_expert_down"][0])

        block = ctx.enter_context(nc.Block())

        @block.sync
        def _(sp):
            xp, xs = a["x_prompt"][0], a["x_sample"][0]
            sp.dma_start(x[:, 0, :], xp[0:P]).then_inc(x_in[0], 16)
            sp.dma_start(gb[:], a["norm_mix_g"][0].partition_broadcast(P)).then_inc(gb_in, 16)
            sp.dma_start(cst[:], a["cst"]).then_inc(cst_in, 16)

            def load(n, src):
                if n >= RA:
                    sp.wait_ge(lo_done, n - RA + 1)
                sp.dma_start(raw_view(n, src), src).then_inc(raw_in[n % RA], 16)
            for t in range(1, 4):
                sp.dma_start(x[:, t, :], xp[t * P:(t + 1) * P]).then_inc(x_in[t], 16)
            sp.dma_start(x[0:LAST, 4, :], xp[SEQ - LAST:SEQ]).then_inc(x_in[4], 16)
            sp.dma_start(x[LAST:P, 4, :], xs).then_inc(x_in[4], 16)
            for n in range(4):
                load(n, ws[n])
            sp.dma_start(stt[0:BUF, :], a["state_pool"][0, 0]).then_inc(st_in, 16)
            sp.dma_start(bg[:], a["b_gate"][0].rearrange("(c p) -> p c", p=P), allow_slow_non_contiguous=True).then_inc(w_small, 16)
            sp.dma_start(psc[:], a["pool_scale"][0].rearrange("(c p) -> p c", p=P), allow_slow_non_contiguous=True).then_inc(w_small, 16)
            sp.dma_start(sbg[:], a["subln_g"][0].rearrange("(p c) -> p c", c=1)).then_inc(w_small, 16)
            for i, n in enumerate(("lambda_q1", "lambda_k1", "lambda_q2", "lambda_k2")):
                sp.dma_start(lamv[:, i, :], a[n][0].partition_broadcast(P)).then_inc(w_small, 16)
            sp.dma_start(wr[:, :, 0:EG], a["w_router_group"][0].rearrange("(k p) g -> p k g", p=P)).then_inc(w_small, 16)
            for g in range(EG):
                sp.dma_start(wr[:, :, EG + EPG * g:EG + EPG * (g + 1)],
                             a["w_router_expert"][0, g].rearrange("(k p) e -> p k e", p=P)).then_inc(w_small, 16)
            sp.dma_start(rb[:, 0:EG], a["b_router_group"][0].partition_broadcast(P)).then_inc(w_small, 16)
            sp.dma_start(rb[:, EG:20], a["b_router_expert"][0].rearrange("g e -> (g e)").partition_broadcast(P)).then_inc(w_small, 16)
            sp.wait_ge(z_done, 1)
            sp.dma_start(lst[0:ROWS * P, 0].rearrange("(r c) -> r c", c=P), zero[0:ROWS, :]).then_inc(z_out, 16)
            for n in range(4, H0):
                load(n, ws[n])
                if n == H0 - 1:
                    sp.wait_ge(ws_act, count(act_jobs, 6))
                    for k, dst in enumerate((o["new_pool_prompt"], o["new_pool_sample"])):
                        sp.dma_start(dst[0, 0], pst[P - BUF:P, k, :]).then_inc(out_done, 16)
            def load_head(n, h, q):
                sp.wait_ge(lo_done, n - RA + 1)
                sp.sem_inc(sp_go, 1)
                for k in range(2):
                    d = rawA[:, (H0 + q) % RA, 384 * k:384 * k + 384].rearrange("p (s c) -> p s c", s=3)
                    sp.dma_start(d, head_source(h, 2 * q + k)).then_inc(raw_h[(H0 + q) % RA], 16)
            for q in range(4):
                load_head(H0 + q, 0, q)
            sp.wait_ge(ws_dve, len(dve_jobs))
            for k in range(2):
                sp.dma_start(ckv[:, k, :], a[("cache_k", "cache_v")[k]][0, 0, :, 0, :]).then_inc(ckv_in, 16)

            def head_loads(h):
                g = h - 1
                for q in range(4):
                    n = H0 + 4 * h + 4 + q
                    if isinstance(h, int) and h == HEADS - 1:
                        load(n, later_source(n))
                    else:
                        load_head(n, h + 1, q)
                    if q == 0:
                        head_out(g)
                        sp.wait_ge(tr_mm, 2 * g + 2)
                        sp.wait_ge(vlo_done, g + 1)
                        sp.sem_inc(sp_go, 1)
                        for k in range(2):
                            sp.dma_start(ckv[:, k, :], a[("cache_k", "cache_v")[k]][0, 0, :, g + 1, :]).then_inc(ckv_in, 16)

            def head_out(g):
                sp.wait_ge(rope_done, g + 1)
                sp.sem_inc(sp_go, 1)
                for j, (dp, ds) in enumerate(((new_k, new_ks), (new_v, new_vs))):
                    c = slice(P * (j + 1), P * (j + 2))
                    sp.dma_start(dp[:, g, :].rearrange("(t p) c -> p t c", p=P), qkv[:, 0:4, c]).then_inc(kv_out, 16)
                    sp.dma_start(ds[:, g, :], qkv[LAST:P, 4, c]).then_inc(kv_out, 16)

            for q in range(4):
                load_head(H0 + 4 + q, 1, q)
            with sp.Fori(1, HEADS - 1) as h:
                head_loads(h)
            head_loads(HEADS - 1)
            head_out(HEADS - 1)
            sp.wait_ge(ws_act, len(act_jobs))
            for n in range(AB0 + 4, O0):
                src = later_source(n)
                load(n, src)
            sp.wait_ge(an_done, 1)
            sp.dma_start(gb[:], a["norm_ffn_g"][0].partition_broadcast(P)).then_inc(gb_in, 16)

            def moe_load(slot, e, c):
                d = rawM[:, slot, :]
                if c < 8:
                    half, q = divmod(c, 4)
                    d = d.rearrange("p (k m n) -> p k m n", k=2, m=2)
                    for m in range(2):
                        src = moe_src[m][e, 2 * P * q:2 * P * (q + 1), 256 * half:256 * (half + 1)]
                        sp.dma_start(d[:, :, m, :], src.rearrange("(k p) n -> p k n", p=P)).then_inc(m_raw[slot], 16)
                else:
                    sp.dma_start(d, moe_src[2][e, P * (c - 8):P * (c - 7), :]).then_inc(m_raw[slot], 16)

            for n in range(O0, NCH):
                load(n, later_source(n))
                if n == O0 + 3:
                    sp.wait_ge(ab_lo, 4)
                for s in range(5 * (n - O0 - 3), min(5 * (n - O0 - 3) + 5, RM - 2)):
                    if s >= 0:
                        moe_load(s, s // 12, s % 12)
            sp.wait_ge(lo_done, NCH)
            for s in (RM - 2, RM - 1):
                moe_load(s, 1, s % 12)

            for t in range(NT):
                sp.wait_ge(h2_done, t + 1)
                if t < 4:
                    sp.dma_start(h2d[t * P:(t + 1) * P], yb[:, t % 2, :]).then_inc(y_out[t % 2], 16)
                else:
                    sp.dma_start(h2d[SEQ:TOK], yb[LAST:P, t % 2, :]).then_inc(y_out[t % 2], 16)
            sp.dma_start(gb[:], a["final_norm_g"].partition_broadcast(P)).then_inc(gb_in, 16)
            sp.wait_ge(sc_in, 16 * 2 * NT)
            sp.dma_start(lsm[:], lst[0:ROWS * P, 0].rearrange("(r c) -> r c", c=P)).then_inc(ls_in, 16)

            def y_store(i, par):
                sp.wait_ge(y_ev, 2 * i + 2)
                sp.sem_inc(sp_go, 1)
                sp.dma_start(yd.rearrange("(r p) d -> r p d", p=P)[i], yb[:, par, :]).then_inc(y_out[par], 16)

            def next_load(slot, e, c, n):
                sp.wait_ge(m_lo, n - RM + 1)
                sp.sem_inc(sp_go, 1)
                moe_load(slot, e, c)

            with sp.Fori(0, EXPERTS // 2 - 1) as ip:
                for par in range(2):
                    for c in range(12):
                        next_load(12 * par + c, 2 * ip + 2 + par, c, 24 * ip + 24 + 12 * par + c)
                    y_store(2 * ip + par, par)
            for c in range(3):
                next_load(c, 0, c, 12 * EXPERTS + c)
            for par in range(2):
                y_store(EXPERTS - 2 + par, par)
            sp.wait_ge(id_done, 1)
            more = sp.value_load(over[0:1, 0:1], min_val=0, max_val=1)
            with sp.If(more > 0):
                with sp.Fori(1, TILES_PER_EXPERT) as j:
                    with sp.Fori(0, EXPERTS // 2) as eh:
                        for par in range(2):
                            for c in range(3 if par == 0 else 0, 12):
                                next_load(12 * par + c, 2 * eh + par, c, 192 * j + 24 * eh + 12 * par + c)
                        nxt = sp.snap((2 * eh + 2) % EXPERTS)
                        for c in range(3):
                            next_load(c, nxt, c, 192 * j + 24 * eh + 24 + c)
                        for par in range(2):
                            y_store(16 * j + 2 * eh + par, par)
                for par in range(2):
                    sp.wait_ge(y_out[par], Y0[par] + 8 * ROWS)
                for c in range(3):
                    sp.wait_ge(m_raw[c], 32 * (ROWS // 2 + 1))
            for t in range(NT):
                sp.wait_ge(f_done, t + 1)
                dst, src = (o["y_prompt"][0, t * P:(t + 1) * P], ob[:, t % 2, :]) if t < 4 else (o["y_sample"][0], ob[LAST:P, 0, :])
                sp.dma_start(dst, src).then_inc(f_out[t % 2], 16)
            sp.wait_ge(f_out[0], 48)
            sp.wait_ge(f_out[1], 32)
            sp.wait_ge(kv_out, 64 * HEADS)
            for c in range(3):
                sp.wait_ge(m_raw[c], 32 * (EXPERTS // 2 + 1))

        @block.gpsimd
        def _(pool):
            pool.memset(zero[:], 0.0).then_inc(z_done, 1)
            pool.wait_ge(z_out, 16)
            pool.wait_ge(ix_done, 1)
            for t in range(NT):
                for k in range(2):
                    pool.indirect_dma_start(lst[:, :], bass.IndirectOffsetOnAxis(ap=tix[:, t, k:k + 1], axis=0),
                                            cst[:, C_TOK + t:C_TOK + t + 1], None).then_inc(sc_in, 16)

            def gather(i, par):
                pool.tensor_copy(idn[:, par:par + 1], idi[:, bass.ds(i, 1)]).then_inc(p_ch, 1)
                pool.wait_ge(p_ch, i + 1)
                pool.sem_inc(p_go, 1)
                pool.indirect_dma_start(xg[:, par, :], None, h2d[:, :],
                                        bass.IndirectOffsetOnAxis(ap=idn[:, par:par + 1], axis=0)).then_inc(g_in[par], 16)
            for par in range(2):
                pool.wait_ge(y_out[par], Y0[par])
            pool.wait_ge(id_done, 1)
            gather(0, 0)
            gather(1, 1)

            def pair(ip):
                for par in range(2):
                    pool.wait_ge(xg_mm, 2 * ip + par + 1)
                    pool.sem_inc(p_go, 1)
                    gather(2 * ip + par + 2, par)
            with pool.Fori(0, EXPERTS // 2) as ip:
                pair(ip)
            more = pool.value_load(over[0:1, 0:1], min_val=0, max_val=1)
            with pool.If(more > 0):
                with pool.Fori(EXPERTS // 2, ROWS // 2) as ip:
                    pair(ip)

            def last_rows(items):
                for par in range(2):
                    pool.wait_ge(y_out[par], Y0[par] + 8 * items)
                for t in range(NT):
                    if t >= 2:
                        pool.wait_ge(f_ms, t - 1)
                    for k in range(2):
                        pool.indirect_dma_start(fy[:, t % 2, k, :], None, yd[0:items * P, :],
                                                bass.IndirectOffsetOnAxis(ap=yidx[:, t, k:k + 1], axis=0)).then_inc(fy_in[t % 2], 16)
            with pool.If(more > 0):
                last_rows(ROWS)
            with pool.If(more < 1):
                last_rows(EXPERTS)

        @block.scalar
        def _(act):
            def hi(n, w=None):
                if H0 <= n < AB0:
                    act.wait_ge(raw_h[n % RA], 32 * ((n - H0) // 4 + 1))
                else:
                    act.wait_ge(*arrival(n))
                if n >= S:
                    act.wait_ge(mm_done, n - S + 1)
                w = words(n)
                nc.scalar.activation(wh[:, n % S, 0:w], rawA[:, n % RA, 0:w], ACT.Copy).then_inc(hi_done, 1)

            split = [0]

            def split_to(n):
                while split[0] <= n:
                    hi(split[0])
                    split[0] += 1

            for t in range(NT):
                act.wait_ge(ms_done, t + 1)
                nc.scalar.activation(rsx[:, t:t + 1], rsx[:, t:t + 1], ACT.Sqrt).then_inc(rt_done, 1)
            for t in range(NT):
                act.wait_ge(xt_mm, t + 1)
                b, n0, c0 = 2 * (t % 4), P if t < 4 else DEC, P * t
                v = ps[:, b:b + 2, :].rearrange("p b (k n) -> p b k n", k=4)[:, :, :, P - n0:P]
                nc.scalar.activation(hTh[:, :, c0:c0 + n0].rearrange("p (b k) n -> p b k n", b=2), v,
                                     ACT.Copy).then_inc(xt_hi, 1)
                split_to(t - 1)
            act.wait_ge(st_mm, 1)
            act.wait_ge(pad_done, 1)
            nc.scalar.activation(U[:, :, BUF + SEQ:US], ps[:, 2, :].rearrange("p (g n) -> p g n", g=4)[:, :, 0:BUF],
                                 ACT.Copy).then_inc(st_ev, 1)
            act.wait_ge(lam_s, 1)
            nc.scalar.activation(lame[:], lame[:], ACT.Exp).then_inc(lam_e, 1)
            act.wait_ge(w_small, 14 * 16)
            for j, (stage, i, chunks) in enumerate(jobs):
                if chunks:
                    split_to(min(chunks[-1] + 3, H0 + 2))
                b = 4 * (j % 2)
                acc = ps[:, b:b + 4, 0:HALF].rearrange("p (c h) n -> p c h n", c=2)
                if stage == "pA":
                    continue
                if stage == "last":
                    act.wait_ge(last_mm, 1)
                else:
                    act.wait_ge(mm_done, chunks[-1] + 1)
                if stage == "u":
                    n1 = SEQ - HALF
                    nc.scalar.activation(U[:, 2 * i:2 * i + 2, BUF:BUF + HALF], acc[:, :, 0, :], ACT.Copy)
                    nc.scalar.activation(U[:, 2 * i:2 * i + 2, BUF + HALF:BUF + SEQ], acc[:, :, 1, 0:n1], ACT.Copy)
                    nc.scalar.activation(U[:, 2 * i:2 * i + 2, US:UW], acc[:, :, 1, n1:HALF], ACT.Copy).then_inc(ws_act, 1)
                elif stage == "gB":
                    for c in range(2):
                        ins = nc.scalar.activation(gB[:, 2 * i + c, :].rearrange("p (h n) -> p h n", h=2), acc[:, c],
                                                   ACT.Sigmoid, bias=bg[:, KD + 2 * i + c:KD + 2 * i + c + 1])
                    ins.then_inc(ws_act, 1)
                    if i == 2:
                        act.wait_ge(pool_done, 1)
                        nc.scalar.activation(ddh[:], dd[:], ACT.Copy).then_inc(dh_done, 1)
                elif stage == "last":
                    nc.scalar.activation(pst[96:P, :, :], ps[96:P, b:b + 2, :], ACT.Copy).then_inc(ws_act, 1)
                elif stage == "pl":
                    for c in range(2):
                        g = 2 * i + c
                        ins = nc.scalar.activation(plh[:, g, :].rearrange("p (h n) -> p h n", h=2), acc[:, c],
                                                   ACT.Copy, scale=psc[:, g:g + 1])
                    ins.then_inc(ws_act, 1)
                elif stage == "gA":
                    if i:
                        act.wait_ge(ws_dve, 2 + i)
                    for c in range(2):
                        ins = nc.scalar.activation(sg[:, c, :].rearrange("p (h n) -> p h n", h=2), acc[:, c],
                                                   ACT.Sigmoid, bias=bg[:, 2 * i + c:2 * i + c + 1])
                    ins.then_inc(ws_act, 1)

            def hi_head(q, n, rnd, w=WH):
                sl = (H0 + q) % S
                if w == WH:
                    act.wait_ge(raw_h[sl], 32 * (rnd + 1))
                else:
                    act.wait_ge(*arrival(n))
                act.wait_ge(mm_done, n - S + 1)
                nc.scalar.activation(wh[:, sl, 0:w], rawA[:, sl, 0:w], ACT.Copy).then_inc(hi_done, 1)

            def evacuate(h):
                for t in range(NT):
                    if t < 4:
                        act.wait_ge(acc_mm, 4 * h + t + 1)
                    else:
                        act.wait_ge(mm_done, H0 + 4 * h + 4)
                    if t == 0 and not (isinstance(h, int) and h == 0):
                        act.wait_ge(kv_out, 64 * h)
                        act.wait_ge(tr_lo, 3 * h)
                        act.wait_ge(vlo_done, h)
                    nc.scalar.activation(qkv[:, t, :], ps[:, t, 0:384], ACT.Copy).then_inc(acc_ev, 1)

            def attend(g, nxt):
                act.wait_ge(acc_ev, NT * (g + 1))
                if not (isinstance(g, int) and g == 0):
                    act.wait_ge(av_mm, NT * g)
                act.wait_ge(ckv_in, 32 * (g + 1))
                nc.scalar.activation(vh[:, 0:NT, :], qkv[:, :, 2 * P:3 * P], ACT.Copy)
                nc.scalar.activation(vh[:, NT, :], ckv[:, 1, :], ACT.Copy).then_inc(vhi_done, 1)
                nxt(3)
                act.wait_ge(tr_mm, 2 * g + 1)
                nc.scalar.activation(qkh[:, :, 0:SEQ], ps[:, 5:7, :], ACT.Copy).then_inc(tr_hi, 1)
                act.wait_ge(tr_mm, 2 * g + 2)
                v = ps[:, 7, 0:2 * P].rearrange("p (m n) -> p m n", m=2)
                nc.scalar.activation(qkh[:, :, SEQ:TOK], v[:, :, LAST:P], ACT.Copy).then_inc(tr_hi, 1)
                nc.scalar.activation(ckh[:], ps[:, 7, 2 * P:3 * P], ACT.Copy).then_inc(tr_hi, 1)
                nxt(4)
                for s in range(NT + 2):
                    if s >= 2:
                        act.wait_ge(av_mm, NT * g + s - 1)
                        nc.scalar.activation(bsq[:], ps[:, 7, 0:P], ACT.Square, scale=BIG_SCALE,
                                             accum_out=ssb[:, s - 2, bass.ds(g, 1)])
                        nc.scalar.activation(att[:, s - 2, g, :], ps[:, 7, 0:P], ACT.Copy).then_inc(av_ev, 1)
                    if 1 <= s <= NT:
                        kb = s if s < NT else 2
                        act.wait_ge(ta_mm, NT * g + s)
                        nc.scalar.activation(ath[:, 0:kb, :], ps[:, 7, 0:kb * P].rearrange("p (k n) -> p k n", k=kb),
                                             ACT.Copy).then_inc(ath_done, 1)
                    if s < NT:
                        n = P * (s + 1) if s < 4 else 2 * P
                        act.wait_ge(nb_done, NT * g + s + 1)
                        if s >= 2:
                            act.wait_ge(am_done, NT * g + s - 1)
                        elif not (isinstance(g, int) and g == 0):
                            act.wait_ge(am_done, NT * g)
                        for m in range(2):
                            ins = nc.scalar.activation(E[:, s % 2, m, 0:n], ps[:, 5 + m, 0:n], ACT.Exp,
                                                       bias=nb[:, s % 2, m:m + 1], scale=SCALE,
                                                       accum_out=esum[:, s % 2, m:m + 1])
                        ins.then_inc(exp_done, 1)
                    if s == 2:
                        nxt(5)
                    if s == 4:
                        nxt(6)

            split_to(H0 + 6)
            act.wait_ge(out_done, 32)
            evacuate(0)

            def head(h, w_next=WH):
                n = H0 + 4 * h
                attend(h - 1, lambda k: hi_head(k % 4, n + k, h + k // 4, WH if k == 3 else w_next))
                evacuate(h)
            with act.Fori(1, HEADS - 1) as h:
                head(h)
            head(HEADS - 1, SLOT)
            split[0] = AB0 + 3
            attend(HEADS - 1, lambda k: split_to(AB0 + 3))

            act.wait_ge(ms_done, NT + 1)
            nc.scalar.activation(rsa[:], rsa[:], ACT.Sqrt).then_inc(rt_done, 1)
            for t in range(NT):
                act.wait_ge(at_mm, t + 1)
                b, n0, c0 = 2 * (t % 4), P if t < 4 else DEC, P * t
                v = ps[:, b:b + 2, :].rearrange("p b (k n) -> p b k n", k=4)[:, :, :, P - n0:P]
                nc.scalar.activation(hTh[:, :, c0:c0 + n0].rearrange("p (b k) n -> p b k n", b=2), v,
                                     ACT.Copy, scale=sbg[:, 0:1]).then_inc(at_hi, 1)
            for m in range(4):
                split_to(AB0 + 2 * m + 4)
                act.wait_ge(ab_sum, m + 1)
                nc.scalar.activation(mh[:, 2 * m:2 * m + 2, :], mA[:, 2 * m:2 * m + 2, :], ACT.Copy).then_inc(ab_hi, 1)
            split_to(NCH - 1)
            for t in range(NT):
                act.wait_ge(ms_done, NT + 2 + t)
                nc.scalar.activation(rsx[:, t:t + 1], rsx[:, t:t + 1], ACT.Sqrt).then_inc(rt_done, 1)
                act.wait_ge(h2_mm, t + 1)
                if t:
                    act.wait_ge(lg_mm, t)
                b = 2 * (t % 2)
                nc.scalar.activation(h2T[:].rearrange("p (b k) n -> p b k n", b=2),
                                     ps[:, b:b + 2, :].rearrange("p b (k n) -> p b k n", k=4), ACT.Copy).then_inc(h2_ev, 1)
            act.wait_ge(gd_done, 1)
            nc.scalar.activation(rt[:, 8:13, :], rt[:, 8:13, :], ACT.Exp).then_inc(ge_done, 1)

            def m_hi_split(n, par, c, rnd, first=False):
                slot = 12 * par + c
                act.wait_ge(m_raw[slot], (32 if c < 8 else 16) * (rnd + 1))
                if first:
                    act.wait_ge(mm_done, NCH)
                else:
                    act.wait_ge(m_mm, n - S + 1)
                nc.scalar.activation(wh[:, c % S, :], rawM[:, slot, :], ACT.Copy).then_inc(m_hi, 1)

            def rows_hi(i, par):
                act.wait_ge(xg_mm, i + 1)
                nc.scalar.activation(xh[:].rearrange("p (b k) n -> p b k n", b=2),
                                     ps[:, 2:4, :].rearrange("p b (k n) -> p b k n", k=4), ACT.Copy).then_inc(xg_hi, 1)

            def item(ip, par):
                i = 2 * ip + par
                n0 = 24 * ip + 12 * par

                def ahead(c):
                    if c < 12:
                        m_hi_split(n0 + c, par, c, ip)
                    else:
                        m_hi_split(n0 + c, 1 - par, c - 12, ip + par)
                for c in range(3, 7):
                    ahead(c)
                for half in range(2):
                    act.wait_ge(m_mm, n0 + 4 * half + 4)
                    act.wait_ge(hid_done, 2 * i + half)
                    nc.scalar.activation(hsl[:, 256 * half:256 * half + 256], ps[:, half, 0:256], ACT.Silu).then_inc(si_done, 1)
                    if half == 0:
                        ahead(7)
                        act.wait_ge(hid_mm, 2 * i + 1)
                        nc.scalar.activation(hh[:, 0:2, :], ps[:, 4, 0:256].rearrange("p (k n) -> p k n", k=2),
                                             ACT.Copy).then_inc(hid_hi, 1)
                        for c in range(8, 11):
                            ahead(c)
                rows_hi(i + 1, 1 - par)
                ahead(11)
                act.wait_ge(hid_mm, 2 * i + 2)
                nc.scalar.activation(hh[:, 2:4, :], ps[:, 4, 256:512].rearrange("p (k n) -> p k n", k=2),
                                     ACT.Copy).then_inc(hid_hi, 1)
                for c in range(12, 15):
                    ahead(c)
                act.wait_ge(m_mm, n0 + 12)
                act.wait_ge(y_out[par], Y0[par] + 16 * ip)
                for b in range(2):
                    nc.scalar.activation(yb[:, par, 512 * b:512 * b + 512], ps[:, 5 + b, :], ACT.Copy).then_inc(y_ev, 1)
            for c in range(3):
                m_hi_split(c, 0, c, 0, first=True)
            rows_hi(0, 0)
            with act.Fori(0, EXPERTS // 2) as ip:
                for par in range(2):
                    item(ip, par)
            more = act.value_load(over[0:1, 0:1], min_val=0, max_val=1)
            with act.If(more > 0):
                with act.Fori(EXPERTS // 2, ROWS // 2) as ip:
                    for par in range(2):
                        item(ip, par)
            for t in range(NT):
                act.wait_ge(f_ms, t + 1)
                nc.scalar.activation(rsx[:, t:t + 1], rsx[:, t:t + 1], ACT.Sqrt).then_inc(f_rt, 1)

        @block.vector
        def _(dve):
            V = nc.vector
            links = [0]

            def link(ins, base=0):
                links[0] += 1
                ins.then_inc(dch, 1)
                dve.wait_ge(dch, base + links[0])

            def lo(n):
                dve.wait_ge(hi_done, n + 1)
                w = words(n)
                V.tensor_tensor(wl[:, n % S, 0:w], rawA[:, n % RA, 0:w], wh[:, n % S, 0:w].bitcast(F32),
                                ALU.subtract).then_inc(lo_done, 1)

            split = [0]

            def split_to(n):
                while split[0] <= n:
                    lo(split[0])
                    split[0] += 1

            def mean_square(src, dst, scratch):
                link(V.scalar_tensor_tensor(out=scratch, in0=src, scalar=1.0, in1=src, op0=ALU.mult, op1=ALU.mult,
                                            accum_out=dst))
                V.tensor_scalar(dst, dst, 1.0 / D, EPS, ALU.mult, ALU.add).then_inc(ms_done, 1)

            V.memset(U[:, :, 0:BUF], 0.0).then_inc(pad_done, 1)
            V.memset(idi[:, ROWS:ROWS + 2], 0)
            for t in range(NT):
                dve.wait_ge(x_in[t], 16 if t < 4 else 32)
                mean_square(x[:, t, :], rsx[:, t:t + 1], sq[:, t % 2, :])
            dve.wait_ge(gb_in, 16)

            def rows_lo(t, half_scale=None):
                b, n0, c0 = 2 * (t % 4), P if t < 4 else DEC, P * t
                v = ps[:, b:b + 2, :].rearrange("p b (k n) -> p b k n", k=4)[:, :, :, P - n0:P]
                oh = hTh[:, :, c0:c0 + n0].bitcast(F32).rearrange("p (b k) n -> p b k n", b=2)
                ol = hTl[:, :, c0:c0 + n0].rearrange("p (b k) n -> p b k n", b=2)
                return v, oh, ol

            for t in range(NT + 1):
                if t < NT:
                    dve.wait_ge(rt_done, t + 1)
                    link(V.reciprocal(rsx[:, t:t + 1], rsx[:, t:t + 1]))
                    if t >= 2:
                        dve.wait_ge(xt_mm, t - 1)
                    V.scalar_tensor_tensor(out=xn[:, t % 2, :], in0=x[:, t, :], scalar=rsx[:, t:t + 1], in1=gb[:],
                                           op0=ALU.mult, op1=ALU.mult).then_inc(xn_done, 1)
                if t:
                    dve.wait_ge(xt_hi, t)
                    v, oh, ol = rows_lo(t - 1)
                    V.tensor_tensor(ol, v, oh, ALU.subtract).then_inc(xt_lo, 1)
                    split_to(t - 2)
            dve.wait_ge(w_small, 14 * 16)
            for i in range(2):
                ins = V.scalar_tensor_tensor(out=lamv[:, 2 * i, :], in0=lamv[:, 2 * i, :], scalar=1.0,
                                             in1=lamv[:, 2 * i + 1, :], op0=ALU.mult, op1=ALU.mult,
                                             accum_out=lame[:, i:i + 1])
            ins.then_inc(lam_s, 1)
            V.tensor_scalar(sbg[:], sbg[:], 1.0 - LAM_INIT, None, ALU.mult)
            dve.wait_ge(lam_e, 1)
            V.scalar_tensor_tensor(out=nlam[:], in0=lame[:, 1:2], scalar=-LAM_INIT, in1=lame[:, 0:1],
                                   op0=ALU.add, op1=ALU.subtract).then_inc(lam_done, 1)

            def pool_steps():
                dve.wait_ge(ws_act, 2)
                dve.wait_ge(st_ev, 1)
                link(V.tensor_tensor(B1[:, :, 1:UW], U[:, :, 1:UW], U[:, :, 0:UW - 1], ALU.add))
                yield
                link(V.tensor_tensor(B2[:, :, 3:UW], B1[:, 1:4, 3:UW], B1[:, 1:4, 1:UW - 2], ALU.add))
                yield
                link(V.tensor_tensor(B1[:, 2:4, 7:UW], B2[:, 1:3, 7:UW], B2[:, 1:3, 3:UW - 4], ALU.add))
                yield
                link(V.tensor_tensor(B2[:, 2, 15:UW], B1[:, 3, 15:UW], B1[:, 3, 7:UW - 8], ALU.add))
                for g, w in enumerate(WINDOWS):
                    sums = B1[:, g, :] if g % 2 == 0 else B2[:, g - 1, :]
                    inv = cst[:, C_INV + BUF * g:C_INV + BUF * (g + 1)]
                    V.tensor_tensor(dd[:, g, 0:BUF], sums[:, BUF:2 * BUF], inv, ALU.mult)
                    V.scalar_tensor_tensor(out=dd[:, g, BUF:SEQ], in0=sums[:, 2 * BUF:BUF + SEQ], scalar=1.0 / w,
                                           in1=U[:, g, 2 * BUF:BUF + SEQ], op0=ALU.mult, op1=ALU.subtract)
                    link(V.scalar_tensor_tensor(out=dd[:, g, SEQ:TOK], in0=sums[:, US:UW], scalar=1.0 / w,
                                                in1=U[:, g, US:UW], op0=ALU.mult, op1=ALU.subtract))
                    ins = V.tensor_tensor(dd[:, g, 0:BUF], dd[:, g, 0:BUF], U[:, g, BUF:2 * BUF], ALU.subtract)
                    if g == NG - 1:
                        ins.then_inc(pool_done, 1)
                    yield

            steps = pool_steps()
            split_to(6)
            for j, (stage, i, chunks) in enumerate(jobs):
                b = 4 * (j % 2)
                acc = ps[:, b:b + 4, 0:HALF].rearrange("p (c h) n -> p c h n", c=2)
                if chunks:
                    split_to(min(chunks[-1] + 3, H0 + 2))
                if stage == "gB" and i < 4:
                    for _ in range(4):
                        next(steps, None)
                if stage == "last":
                    dve.wait_ge(dh_done, 1)
                    V.tensor_tensor(ddl[:], dd[:], ddh[:].bitcast(F32), ALU.subtract).then_inc(dl_done, 1)
                if stage == "pl":
                    dve.wait_ge(ws_act, count(act_jobs, j))
                    for c in range(2):
                        g = 2 * i + c
                        ins = V.scalar_tensor_tensor(out=pll[:, g, :].rearrange("p (h n) -> p h n", h=2), in0=acc[:, c],
                                                     scalar=psc[:, g:g + 1],
                                                     in1=plh[:, g, :].bitcast(F32).rearrange("p (h n) -> p h n", h=2),
                                                     op0=ALU.mult, op1=ALU.subtract)
                    ins.then_inc(ws_dve, 1)
                if stage == "pA":
                    dve.wait_ge(ws_act, count(act_jobs, j))
                    dve.wait_ge(mm_done, chunks[-1] + 1)
                    V.tensor_tensor(mA[:, 2 * i:2 * i + 2, :].rearrange("p c (h n) -> p c h n", h=2), acc,
                                    sg[:].rearrange("p c (h n) -> p c h n", h=2), ALU.mult).then_inc(ws_dve, 1)

            def lo_head(q, n, w=WH):
                sl = (H0 + q) % S
                dve.wait_ge(hi_done, n + 1)
                V.tensor_tensor(wl[:, sl, 0:w], rawA[:, sl, 0:w], wh[:, sl, 0:w].bitcast(F32),
                                ALU.subtract).then_inc(lo_done, 1)

            per_head = 1 + 5 * NT

            def attend(g, base, nxt):
                def lk(ins):
                    link(ins, base)
                links[0] = 0
                v = qkv[:, :, 0:256].rearrange("p t (g d) -> p t g d", g=4)
                x1, x2 = v[:, :, :, 0:8], v[:, :, :, 8:16]
                cos = cst[:, C_COS:C_COS + 160].rearrange("p (t g d) -> p t g d", t=NT, g=4)
                sin = cst[:, C_SIN:C_SIN + 160].rearrange("p (t g d) -> p t g d", t=NT, g=4)
                tmp = [rot[:, r, :].rearrange("p (t g d) -> p t g d", t=NT, g=4) for r in range(4)]
                dve.wait_ge(acc_ev, NT * (g + 1))
                V.tensor_tensor(tmp[0], x1, cos, ALU.mult)
                V.tensor_tensor(tmp[1], x2, sin, ALU.mult)
                V.tensor_tensor(tmp[2], x2, cos, ALU.mult)
                lk(V.tensor_tensor(tmp[3], x1, sin, ALU.mult))
                V.tensor_tensor(x1, tmp[0], tmp[1], ALU.subtract)
                V.tensor_tensor(x2, tmp[2], tmp[3], ALU.add).then_inc(rope_done, 1)
                dve.wait_ge(vhi_done, g + 1)
                V.tensor_tensor(vl[:, 0:NT, :], qkv[:, :, 2 * P:3 * P], vh[:, 0:NT, :].bitcast(F32), ALU.subtract)
                V.tensor_tensor(vl[:, NT, :], ckv[:, 1, :], vh[:, NT, :].bitcast(F32), ALU.subtract).then_inc(vlo_done, 1)
                nxt(3)
                dve.wait_ge(tr_hi, 3 * g + 1)
                V.tensor_tensor(qkl[:, :, 0:SEQ], ps[:, 5:7, :], qkh[:, :, 0:SEQ].bitcast(F32), ALU.subtract).then_inc(tr_lo, 1)
                dve.wait_ge(tr_hi, 3 * g + 3)
                w = ps[:, 7, 0:2 * P].rearrange("p (m n) -> p m n", m=2)
                V.tensor_tensor(qkl[:, :, SEQ:TOK], w[:, :, LAST:P], qkh[:, :, SEQ:TOK].bitcast(F32),
                                ALU.subtract).then_inc(tr_lo, 1)
                V.tensor_tensor(ckl[:], ps[:, 7, 2 * P:3 * P], ckh[:].bitcast(F32), ALU.subtract).then_inc(tr_lo, 1)
                nxt(4)
                for s in range(NT + 2):
                    if 1 <= s <= NT:
                        t = s - 1
                        n = P * (t + 1) if t < 4 else 2 * P
                        dve.wait_ge(exp_done, NT * g + s)
                        lk(V.reciprocal(rinv[:, t % 2, :], esum[:, t % 2, :]))
                        V.tensor_tensor(rinv[:, t % 2, 1:2], rinv[:, t % 2, 1:2], nlam[:], ALU.mult)
                        lk(V.tensor_scalar(E[:, t % 2, 0, 0:n], E[:, t % 2, 0, 0:n], rinv[:, t % 2, 0:1], None, ALU.mult))
                        if t:
                            dve.wait_ge(ta_mm, NT * g + t)
                        V.scalar_tensor_tensor(out=Am[:, 0:n], in0=E[:, t % 2, 1, 0:n], scalar=rinv[:, t % 2, 1:2],
                                               in1=E[:, t % 2, 0, 0:n], op0=ALU.mult, op1=ALU.add).then_inc(am_done, 1)
                    if s < NT:
                        n = P * (s + 1) if s < 4 else 2 * P
                        dve.wait_ge(sc_mm, NT * g + s + 1)
                        lk(V.tensor_reduce(mx[:, s % 2, :], ps[:, 5:7, 0:n], AX.X, ALU.max))
                        V.tensor_scalar(nb[:, s % 2, :], mx[:, s % 2, :], -SCALE, None, ALU.mult).then_inc(nb_done, 1)
                    if 1 <= s <= NT:
                        kb = s if s < NT else 2
                        dve.wait_ge(ath_done, NT * g + s)
                        V.tensor_tensor(atl[:, 0:kb, :], ps[:, 7, 0:kb * P].rearrange("p (k n) -> p k n", k=kb),
                                        ath[:, 0:kb, :].bitcast(F32), ALU.subtract).then_inc(atl_done, 1)
                    if s >= 2:
                        dve.wait_ge(av_ev, NT * g + s - 1)
                        lk(V.tensor_scalar(asq[:, 0, :], att[:, s - 2, g, :], CLAMP, -CLAMP, ALU.min, ALU.max))
                        ins = V.scalar_tensor_tensor(out=asq[:, 1, :], in0=asq[:, 0, :], scalar=1.0,
                                                     in1=asq[:, 0, :], op0=ALU.mult, op1=ALU.mult,
                                                     accum_out=ssa[:, s - 2, bass.ds(g, 1)])
                        lk(ins)
                    if s == 2:
                        nxt(5)
                    if s == 4:
                        nxt(6)
                assert links[0] == per_head

            dve.wait_ge(lam_done, 1)
            dve.wait_ge(out_done, 32)
            split_to(H0 + 6)
            d0 = links[0]

            def head(h, w_next=WH):
                n = H0 + 4 * h
                attend(h - 1, d0 + per_head * (h - 1), lambda k: lo_head(k % 4, n + k, WH if k == 3 else w_next))
            with dve.Fori(1, HEADS - 1) as h:
                head(h)
            head(HEADS - 1, SLOT)
            split[0] = AB0 + 3
            attend(HEADS - 1, d0 + per_head * (HEADS - 1), lambda k: split_to(AB0 + 3))
            links[0] = d0 + per_head * HEADS

            big, one = BIG_SUM / (BIG_SCALE ** -2), 2.0 ** 128 * BIG_SCALE ** 2
            link(V.tensor_scalar(fin[:], ssb[:], big, None, ALU.is_ge))
            link(V.tensor_scalar(isb[:], ssb[:], one, 2.0 ** -40 * BIG_SCALE ** -2 / P, ALU.min, ALU.mult))
            link(V.tensor_tensor(isb[:], isb[:], fin[:], ALU.mult))
            link(V.tensor_scalar(rsa[:], ssa[:], 2.0 ** -40 / P, 2.0 ** -40 * EPS, ALU.mult, ALU.add))
            link(V.tensor_scalar(fin[:], fin[:], -1.0, 1.0, ALU.mult, ALU.add))
            link(V.tensor_tensor(rsa[:], rsa[:], fin[:], ALU.mult))
            link(V.tensor_tensor(rsa[:], rsa[:], isb[:], ALU.add))
            V.tensor_scalar(fin[:], ssb[:], one, 2.0 ** -20, ALU.is_lt, ALU.mult).then_inc(ms_done, 1)
            dve.wait_ge(rt_done, NT + 1)
            link(V.reciprocal(rsa[:], rsa[:]))
            link(V.tensor_tensor(rsa[:], rsa[:], fin[:], ALU.mult))
            for t in range(NT + 1):
                if t < NT:
                    V.tensor_tensor(att[:, t], att[:, t], rsa[:, t, :].unsqueeze(2).broadcast_to([P, HEADS, P]),
                                    ALU.mult).then_inc(an_done, 1)
                if t:
                    dve.wait_ge(at_hi, t)
                    v, oh, ol = rows_lo(t - 1)
                    V.scalar_tensor_tensor(out=ol, in0=v, scalar=sbg[:, 0:1], in1=oh, op0=ALU.mult,
                                           op1=ALU.subtract).then_inc(at_lo, 1)
            for m in range(4):
                b = 4 * (m % 2)
                acc = ps[:, b:b + 4, 0:HALF].rearrange("p (c h) n -> p c h n", c=2)
                four = lambda r: r.rearrange("p c (h n) -> p c h n", h=2)
                split_to(AB0 + 2 * m + 4)
                dve.wait_ge(mm_done, AB0 + 2 * m + 2)
                link(V.tensor_tensor(four(gt[:]), acc, four(gB[:, 2 * m:2 * m + 2, :]), ALU.mult))
                V.tensor_tensor(mA[:, 2 * m:2 * m + 2, :], mA[:, 2 * m:2 * m + 2, :], gt[:], ALU.add).then_inc(ab_sum, 1)
                dve.wait_ge(ab_hi, m + 1)
                V.tensor_tensor(ml[:, 2 * m:2 * m + 2, :], mA[:, 2 * m:2 * m + 2, :],
                                mh[:, 2 * m:2 * m + 2, :].bitcast(F32), ALU.subtract).then_inc(ab_lo, 1)
            for m in range(2):
                split_to(min(O0 + 4 * m + 6, NCH - 1))
                for t in range(NT):
                    if t < 4:
                        dve.wait_ge(o_mm, 4 * m + t + 1)
                    else:
                        dve.wait_ge(mm_done, O0 + 4 * m + 4)
                    xs = x[:, t, 512 * m:512 * m + 512]
                    V.tensor_tensor(xs, ps[:, (NT * m + t) % 8, :], xs, ALU.add).then_inc(o_ev, 1)

            dve.wait_ge(gb_in, 32)
            dve.wait_ge(o_ev, 2 * NT)
            for t in range(NT):
                mean_square(x[:, t, :], rsx[:, t:t + 1], xg[:, 0, :])
            for t in range(NT):
                dve.wait_ge(rt_done, NT + 2 + t)
                link(V.reciprocal(rsx[:, t:t + 1], rsx[:, t:t + 1]))
                if t >= 2:
                    dve.wait_ge(y_out[t % 2], 16 * (t // 2))
                    dve.wait_ge(h2_mm, t - 1)
                V.scalar_tensor_tensor(out=yb[:, t % 2, :], in0=x[:, t, :], scalar=rsx[:, t:t + 1], in1=gb[:],
                                       op0=ALU.mult, op1=ALU.mult).then_inc(h2_done, 1)
            dve.wait_ge(lg_mm, NT)
            bc = lambda r, n: r.unsqueeze(2).broadcast_to([P, NT, n])
            link(V.tensor_tensor(lg[:], ps[:, 4, 0:NT * 20].rearrange("p (t n) -> p t n", t=NT),
                                 rb[:].unsqueeze(1).broadcast_to([P, NT, 20]), ALU.add))
            iota = cst[:, C_IOTA:C_IOTA + EXPERTS].unsqueeze(1).broadcast_to([P, NT, EXPERTS])
            gl, el = lg[:, :, 0:EG], lg[:, :, EG:20]

            def first_max(src, n, m, onehot, scratch):
                link(V.tensor_reduce(m, src, AX.X, ALU.max))
                link(V.tensor_tensor(scratch, src, bc(m, n), ALU.is_equal))
                link(V.tensor_tensor(scratch, scratch, iota[:, :, 0:n], ALU.mult))
                link(V.tensor_reduce(rt[:, 15, :], scratch, AX.X, ALU.min))
                link(V.tensor_tensor(onehot, iota[:, :, 0:n], bc(rt[:, 15, :], n), ALU.is_equal))
            gmax, m1, m2 = rt[:, 0, :], rt[:, 1, :], rt[:, 2, :]
            first_max(gl, EG, gmax, ra[0][:, :, 0:EG], ra[1][:, :, 0:EG])
            link(V.tensor_scalar(ra[0][:, :, 0:EG], ra[0][:, :, 0:EG], -NEG, NEG, ALU.mult, ALU.add))
            link(V.tensor_tensor(ra[1][:].rearrange("p t (g e) -> p t g e", g=EG), el.rearrange("p t (g e) -> p t g e", g=EG),
                                 ra[0][:, :, 0:EG].unsqueeze(3).broadcast_to([P, NT, EG, EPG]), ALU.add))
            first_max(ra[1][:], EXPERTS, m1, ra[2][:], ra[3][:])
            link(V.scalar_tensor_tensor(out=ra[4][:], in0=ra[2][:], scalar=2 * NEG, in1=ra[1][:], op0=ALU.mult, op1=ALU.add))
            first_max(ra[4][:], EXPERTS, m2, ra[5][:], ra[3][:])
            V.tensor_tensor(rt[:, 8:12, :].rearrange("p g t -> p t g"), gl, bc(gmax, EG), ALU.subtract)
            V.tensor_tensor(rt[:, 12, :], m2, m1, ALU.subtract).then_inc(gd_done, 1)
            link(V.tensor_tensor(ra[1][:], ra[2][:], ra[5][:], ALU.add))
            V.tensor_tensor(ra[1][:], ra[1][:], bc(cst[:, C_VAL:C_VAL + NT], EXPERTS), ALU.mult).then_inc(sel_done, 1)
            dve.wait_ge(ge_done, 1)
            link(V.tensor_reduce(rt[:, 3, :], rt[:, 8:12, :].rearrange("p g t -> p t g"), AX.X, ALU.add))
            link(V.tensor_scalar(rt[:, 4, :], rt[:, 12, :], 1.0, None, ALU.add))
            link(V.tensor_tensor(rt[:, 4, :], rt[:, 4, :], rt[:, 3, :], ALU.mult))
            link(V.reciprocal(rt[:, 4, :], rt[:, 4, :]))
            V.tensor_copy(wgt[:, :, 0], rt[:, 4, :])
            V.tensor_tensor(wgt[:, :, 1], rt[:, 4, :], rt[:, 12, :], ALU.mult)
            dve.wait_ge(pos_mm, 1)
            pos = ps[:, 5, 0:NT * EXPERTS].rearrange("p (t e) -> p t e", t=NT)
            link(V.tensor_tensor(ra[0][:], pos, cst[:, C_BASE:C_BASE + EXPERTS].unsqueeze(1).broadcast_to([P, NT, EXPERTS]), ALU.add))
            for j in range(1, TILES_PER_EXPERT):
                link(V.tensor_scalar(ra[3][:], pos, float(P * j), float((EXPERTS - 1) * P), ALU.is_ge, ALU.mult))
                link(V.tensor_tensor(ra[0][:], ra[0][:], ra[3][:], ALU.add))
            for k, oh in enumerate((ra[2], ra[5])):
                link(V.tensor_tensor(ra[3][:], oh[:], ra[0][:], ALU.mult))
                link(V.tensor_reduce(rt[:, 5 + k, :], ra[3][:], AX.X, ALU.add))
                link(V.tensor_tensor(rt[:, 5 + k, :], rt[:, 5 + k, :], cst[:, C_VAL:C_VAL + NT], ALU.mult))
                V.tensor_copy(yidx[:, :, k], rt[:, 5 + k, :])
                link(V.tensor_tensor(rt[:, 5 + k, :], rt[:, 5 + k, :],
                                     cst[:, C_TRASH:C_TRASH + 10].rearrange("p (t k) -> p t k", k=2)[:, :, k], ALU.add))
                ins = V.tensor_copy(tix[:, :, k], rt[:, 5 + k, :])
            ins.then_inc(ix_done, 1)
            link(V.tensor_reduce(rt[:, 7, 0:1], ps[:, 5, 80:96], AX.X, ALU.max))
            V.tensor_scalar(over[:], rt[:, 7, 0:1], float(P), None, ALU.is_gt)
            dve.wait_ge(ls_mm, 1)
            V.tensor_copy(idi[:, 0:ROWS], ps[:, 6, 0:ROWS]).then_inc(id_done, 1)

            def item(ip, par):
                i = 2 * ip + par
                n0 = 24 * ip + 12 * par

                def ahead(c):
                    slot = (12 * par + c) % RM
                    dve.wait_ge(m_hi, n0 + c + 1)
                    V.tensor_tensor(wl[:, c % S, :], rawM[:, slot, :], wh[:, c % S, :].bitcast(F32),
                                    ALU.subtract).then_inc(m_lo, 1)
                for c in range(3, 7):
                    ahead(c)
                for half in range(2):
                    hs = slice(256 * half, 256 * half + 256)
                    kk = slice(2 * half, 2 * half + 2)
                    dve.wait_ge(si_done, 2 * i + half + 1)
                    V.tensor_tensor(hid[:, hs], ps[:, half, 256:512], hsl[:, hs], ALU.mult).then_inc(hid_done, 1)
                    if half == 0:
                        ahead(7)
                    else:
                        rows(i + 1)
                        ahead(11)
                    dve.wait_ge(hid_hi, 2 * i + half + 1)
                    V.tensor_tensor(hl[:, kk, :], ps[:, 4, hs].rearrange("p (k n) -> p k n", k=2),
                                    hh[:, kk, :].bitcast(F32), ALU.subtract).then_inc(hid_lo, 1)
                    if half == 0:
                        for c in range(8, 11):
                            ahead(c)
                for c in range(12, 15):
                    ahead(c)

            def rows(i):
                dve.wait_ge(xg_hi, i + 1)
                V.tensor_tensor(xl[:].rearrange("p (b k) n -> p b k n", b=2),
                                ps[:, 2:4, :].rearrange("p b (k n) -> p b k n", k=4),
                                xh[:].bitcast(F32).rearrange("p (b k) n -> p b k n", b=2), ALU.subtract).then_inc(xg_lo, 1)
            for c in range(3):
                dve.wait_ge(m_hi, c + 1)
                V.tensor_tensor(wl[:, c, :], rawM[:, c, :], wh[:, c, :].bitcast(F32), ALU.subtract).then_inc(m_lo, 1)
            rows(0)
            with dve.Fori(0, EXPERTS // 2) as ip:
                for par in range(2):
                    item(ip, par)
            more = dve.value_load(over[0:1, 0:1], min_val=0, max_val=1)
            with dve.If(more > 0):
                with dve.Fori(EXPERTS // 2, ROWS // 2) as ip:
                    for par in range(2):
                        item(ip, par)

            dve.wait_ge(gb_in, 48)
            for t in range(NT):
                xt = x[:, t, :]
                dve.wait_ge(fy_in[t % 2], 32 * (t // 2 + 1))
                for k in range(2):
                    link(V.scalar_tensor_tensor(out=xt, in0=fy[:, t % 2, k, :], scalar=wgt[:, t, k:k + 1], in1=xt,
                                                op0=ALU.mult, op1=ALU.add))
                link(V.scalar_tensor_tensor(out=fsq[:], in0=xt, scalar=1.0, in1=xt, op0=ALU.mult, op1=ALU.mult,
                                            accum_out=rsx[:, t:t + 1]))
                V.tensor_scalar(rsx[:, t:t + 1], rsx[:, t:t + 1], 1.0 / D, EPS, ALU.mult, ALU.add).then_inc(f_ms, 1)
                dve.wait_ge(f_rt, t + 1)
                link(V.reciprocal(rsx[:, t:t + 1], rsx[:, t:t + 1]))
                if t >= 2:
                    dve.wait_ge(f_out[t % 2], 16 * (t // 2))
                V.scalar_tensor_tensor(out=ob[:, t % 2, :], in0=xt, scalar=rsx[:, t:t + 1], in1=gb[:],
                                       op0=ALU.mult, op1=ALU.mult).then_inc(f_done, 1)

        @block.tensor
        def _(pe):
            T = nc.tensor

            def three(out, sh, sl, mh_, ml_, start, stop, **kw):
                T.matmul(out, sh, mh_, start=start, stop=False, **kw)
                T.matmul(out, sh, ml_, start=False, stop=False, **kw)
                return T.matmul(out, sl, mh_, start=False, stop=stop, **kw)

            pe.wait_ge(cst_in, 16)
            for t in range(NT):
                pe.wait_ge(xn_done, t + 1)
                if t >= 4:
                    pe.wait_ge(xt_lo, t - 3)
                for k in range(KD):
                    ins = T.transpose(ps[:, 2 * (t % 4) + k // 4, P * (k % 4):P * (k % 4 + 1)],
                                      xn[:, t % 2, P * k:P * k + P], id_m)
                ins.then_inc(xt_mm, 1)
            pe.wait_ge(st_in, 16)
            pe.wait_ge(xt_lo, 2)
            for g in range(NG):
                ins = T.transpose(ps[:, 2, P * g:P * g + BUF], stt[0:BUF, P * g:P * g + P], cst[0:BUF, C_ID:C_ID + BUF])
            ins.then_inc(st_mm, 1)
            pe.wait_ge(xt_lo, NT)
            pe.wait_ge(st_ev, 1)

            def stationary(chunk_ids, banks, rhs_h, rhs_l, k_first, k_last):
                k = k_first
                for n in chunk_ids:
                    pe.wait_ge(lo_done, n + 1)
                    sl = n % S
                    for kk in range(4):
                        for c in range(2):
                            wc = slice(256 * kk + P * c, 256 * kk + P * (c + 1))
                            for h in range(2):
                                tc = slice(HALF * h, HALF * (h + 1))
                                ins = three(ps[:, banks + 2 * c + h, 0:HALF], wh[:, sl, wc], wl[:, sl, wc],
                                            rhs_h[:, k, tc], rhs_l[:, k, tc], k == 0, k == k_last)
                        k += 1
                    ins.then_inc(mm_done, 1)
                return ins

            for j, (stage, i, chunks) in enumerate(jobs):
                b = 4 * (j % 2)
                if j >= 2:
                    pe.wait_ge(ws_act, count(act_jobs, j - 2))
                    if count(dve_jobs, j - 2):
                        pe.wait_ge(ws_dve, count(dve_jobs, j - 2))
                if stage in ("u", "gB", "gA"):
                    stationary(chunks, b, hTh, hTl, 0, KD - 1)
                elif stage == "pA":
                    stationary(chunks, b, plh, pll, 0, NG - 1)
                elif stage == "last":
                    for k, c1 in enumerate((BUF + SEQ, UW)):
                        for g in range(NG):
                            ins = T.transpose(ps[:, b + k, P * g:P * g + P], U[:, g, c1 - P:c1], id_m)
                    ins.then_inc(last_mm, 1)
                else:
                    pe.wait_ge(lo_done, chunks[0] + 1)
                    pe.wait_ge(dl_done, 1)
                    sl = chunks[0] % S
                    for c in range(2):
                        wc = slice(P * (2 * i + c), P * (2 * i + c + 1))
                        for h in range(2):
                            tc = slice(HALF * h, HALF * (h + 1))
                            ins = three(ps[:, b + 2 * c + h, 0:HALF], wh[:, sl, wc], wl[:, sl, wc],
                                        ddh[:, 2 * i + c, tc], ddl[:, 2 * i + c, tc], True, True)
                    if i == 1:
                        ins.then_inc(mm_done, 1)

            def project(h, j):
                n = H0 + 4 * h + j // 2
                sl, k = (H0 + j // 2) % S, j % 2
                if k == 0:
                    pe.wait_ge(lo_done, n + 1)
                wc = slice(384 * k, 384 * k + 384)
                for t in range(NT):
                    if j == 0:
                        if isinstance(h, int) and h == 0:
                            if t == 0:
                                pe.wait_ge(ws_act, len(act_jobs))
                                pe.wait_ge(ws_dve, len(dve_jobs))
                        else:
                            pe.wait_ge(acc_ev, NT * (h - 1) + t + 1)
                    ins = three(ps[:, t, 0:384], hTh[:, j, col(t)], hTl[:, j, col(t)], wh[:, sl, wc], wl[:, sl, wc],
                                j == 0, j == KD - 1)
                    if j == KD - 1 and t < 4:
                        ins.then_inc(acc_mm, 1)
                if k == 1:
                    ins.then_inc(mm_done, 1)

            def turn(g):
                pe.wait_ge(rope_done, g + 1)
                if not (isinstance(g, int) and g == 0):
                    pe.wait_ge(av_ev, NT * g)
                for m in range(2):
                    for t in range(4):
                        ins = T.transpose(ps[:, 5 + m, P * t:P * t + P], qkv[:, t, P * m:P * m + P], id_m)
                ins.then_inc(tr_mm, 1)
                for m in range(2):
                    T.transpose(ps[:, 7, P * m:P * m + P], qkv[:, 4, P * m:P * m + P], id_m)
                pe.wait_ge(ckv_in, 32 * (g + 1))
                T.transpose(ps[:, 7, 2 * P:3 * P], ckv[:, 0, :], id_m).then_inc(tr_mm, 1)

            def scores(g, t):
                if t == 0:
                    pe.wait_ge(tr_lo, 3 * (g + 1))
                else:
                    pe.wait_ge(exp_done, NT * g + t)
                for m in range(2):
                    r = slice(HD * m, HD * m + HD)
                    qh, ql, out = qkh[r, 0, col(t)], qkl[r, 0, col(t)], ps[:, 5 + m, :]
                    neg = C_NEGH if t < 4 else C_NEGA
                    if t < 4:
                        n = P * (t + 1)
                        keys, hidden, kw = (out[:, 0:n], qkh[r, 1, 0:n], qkl[r, 1, 0:n]), out[:, n - CHUNK:n], {}
                    else:
                        three(out[:, 0:P], qh, ql, ckh[r, :], ckl[r, :], True, True)
                        keys, hidden = (out[:, P:2 * P], qkh[r, 1, col(4)], qkl[r, 1, col(4)]), out[:, P:P + LAST]
                        kw = dict(skip_group_check=True)
                    width = CHUNK if t < 4 else LAST
                    T.matmul(keys[0], qh, keys[1], start=t < 4, stop=False, **kw)
                    T.matmul(hidden, cst[0:1, neg:neg + P], cst[0:1, C_ONE:C_ONE + width], start=False, stop=False, **kw)
                    T.matmul(keys[0], qh, keys[2], start=False, stop=False, **kw)
                    ins = T.matmul(keys[0], ql, keys[1], start=False, stop=True, **kw)
                ins.then_inc(sc_mm, 1)

            def turn_probs(g, t):
                pe.wait_ge(am_done, NT * g + t + 1)
                if t:
                    pe.wait_ge(av_ev, NT * g + t)
                for kb in range(t + 1 if t < 4 else 2):
                    ins = T.transpose(ps[:, 7, P * kb:P * kb + P], Am[:, P * kb:P * kb + P], id_m)
                ins.then_inc(ta_mm, 1)

            def values(g, t):
                pe.wait_ge(atl_done, NT * g + t + 1)
                vs = range(t + 1) if t < 4 else (NT, 4)
                for kb, v in enumerate(vs):
                    ins = three(ps[:, 7, 0:P], ath[:, kb, :], atl[:, kb, :], vh[:, v, :], vl[:, v, :],
                                kb == 0, kb == len(vs) - 1)
                ins.then_inc(av_mm, 1)

            def attend_step(g, s):
                if s >= 2:
                    values(g, s - 2)
                if s < NT:
                    scores(g, s)
                if 1 <= s <= NT:
                    turn_probs(g, s - 1)

            for j in range(KD):
                project(0, j)

            def head(h):
                project(h, 0)
                project(h, 1)
                turn(h - 1)
                project(h, 2)
                for s in range(NT + 2):
                    attend_step(h - 1, s)
                    if s + 3 < KD:
                        project(h, s + 3)
            with pe.Fori(1, HEADS - 1) as h:
                head(h)
            head(HEADS - 1)
            turn(HEADS - 1)
            for s in range(NT + 2):
                attend_step(HEADS - 1, s)

            for t in range(NT):
                pe.wait_ge(an_done, t + 1)
                if t == 0:
                    pe.wait_ge(acc_ev, NT * HEADS)
                if t == 2:
                    pe.wait_ge(exp_done, NT * HEADS)
                if t == 3:
                    pe.wait_ge(av_ev, NT * HEADS)
                if t == 4:
                    pe.wait_ge(at_lo, 1)
                for k in range(KD):
                    ins = T.transpose(ps[:, 2 * (t % 4) + k // 4, P * (k % 4):P * (k % 4 + 1)], att[:, t, k, :], id_m)
                ins.then_inc(at_mm, 1)
            pe.wait_ge(at_lo, NT)
            for m in range(4):
                if m >= 2:
                    pe.wait_ge(ab_lo, m - 1)
                stationary([AB0 + 2 * m, AB0 + 2 * m + 1], 4 * (m % 2), hTh, hTl, 0, KD - 1)
            pe.wait_ge(ab_lo, 4)
            for m in range(2):
                for q in range(4):
                    n = O0 + 4 * m + q
                    pe.wait_ge(lo_done, n + 1)
                    for kk in range(2):
                        wc = slice(512 * kk, 512 * kk + 512)
                        for t in range(NT):
                            if m and q == kk == 0 and t >= 3:
                                pe.wait_ge(o_ev, t - 2)
                            ins = three(ps[:, (NT * m + t) % 8, :], mh[:, 2 * q + kk, col(t)], ml[:, 2 * q + kk, col(t)],
                                        wh[:, n % S, wc], wl[:, n % S, wc], q == kk == 0, q == 3 and kk == 1)
                            if q == 3 and kk == 1 and t < 4:
                                ins.then_inc(o_mm, 1)
                    ins.then_inc(mm_done, 1)

            def turn_rows(t):
                pe.wait_ge(h2_done, t + 1)
                if t >= 2:
                    pe.wait_ge(h2_ev, t - 1)
                for k in range(KD):
                    ins = T.transpose(ps[:, 2 * (t % 2) + k // 4, P * (k % 4):P * (k % 4 + 1)],
                                      yb[:, t % 2, P * k:P * k + P], id_m)
                ins.then_inc(h2_mm, 1)
            pe.wait_ge(o_ev, 2 * NT)
            turn_rows(0)
            for t in range(NT):
                if t + 1 < NT:
                    turn_rows(t + 1)
                pe.wait_ge(h2_ev, t + 1)
                for k in range(KD):
                    ins = T.matmul(ps[:, 4, 20 * t:20 * t + 20], h2T[:, k, :], wr[:, k, :], start=(k == 0), stop=(k == KD - 1))
                ins.then_inc(lg_mm, 1)
            pe.wait_ge(sel_done, 1)
            ones, tri = cst[:, C_ONE:C_ONE + P], cst[:, C_TRI:C_TRI + P]
            for t in range(NT + 1):
                for j in range(min(t + 1, NT)):
                    ins = T.matmul(ps[:, 5, 16 * t:16 * t + 16], tri if j == t else ones, ra[1][:, j, :],
                                   start=(j == 0), stop=(j == min(t, NT - 1)))
            ins.then_inc(pos_mm, 1)
            pe.wait_ge(ls_in, 16)
            T.transpose(ps[:, 6, 0:ROWS], lsm[:], cst[0:ROWS, C_ID:C_ID + ROWS]).then_inc(ls_mm, 1)

            def gathered(ip, par, i):
                pe.wait_ge(g_in[par], 16 * (ip + 1))
                pe.wait_ge(xg_lo, i)
                for k in range(KD):
                    ins = T.transpose(ps[:, 2 + k // 4, P * (k % 4):P * (k % 4 + 1)], xg[:, par, P * k:P * k + P], id_m)
                ins.then_inc(xg_mm, 1)

            def item(ip, par):
                i = 2 * ip + par
                n0 = 24 * ip + 12 * par

                def up(c):
                    pe.wait_ge(m_lo, n0 + c + 1)
                    for kk in range(2):
                        k = 2 * (c % 4) + kk
                        wc = slice(512 * kk, 512 * kk + 512)
                        ins = three(ps[:, c // 4, :], xh[:, k, :], xl[:, k, :], wh[:, c % S, wc], wl[:, c % S, wc],
                                    k == 0, k == KD - 1)
                    ins.then_inc(m_mm, 1)

                def turn_hidden(half):
                    pe.wait_ge(hid_done, 2 * i + half + 1)
                    for k in range(2 * half, 2 * half + 2):
                        ins = T.transpose(ps[:, 4, P * k:P * k + P], hid[:, P * k:P * k + P], id_m)
                    ins.then_inc(hid_mm, 1)

                def down(k):
                    c = 8 + k
                    pe.wait_ge(m_lo, n0 + c + 1)
                    for b in range(2):
                        wc = slice(512 * b, 512 * b + 512)
                        ins = three(ps[:, 5 + b, :], hh[:, k, :], hl[:, k, :], wh[:, c % S, wc], wl[:, c % S, wc],
                                    k == 0, k == 3)
                    ins.then_inc(m_mm, 1)
                pe.wait_ge(xg_lo, i + 1)
                pe.wait_ge(hid_done, 2 * i)
                for c in range(6):
                    up(c)
                turn_hidden(0)
                up(6)
                up(7)
                pe.wait_ge(hid_lo, 2 * i + 1)
                pe.wait_ge(y_ev, 2 * i)
                down(0)
                gathered(ip + par, 1 - par, i + 1)
                turn_hidden(1)
                down(1)
                pe.wait_ge(hid_lo, 2 * i + 2)
                down(2)
                down(3)
            pe.wait_ge(id_done, 1)
            gathered(0, 0, 0)
            with pe.Fori(0, EXPERTS // 2) as ip:
                for par in range(2):
                    item(ip, par)
            more = pe.value_load(over[0:1, 0:1], min_val=0, max_val=1)
            with pe.If(more > 0):
                with pe.Fori(EXPERTS // 2, ROWS // 2) as ip:
                    for par in range(2):
                        item(ip, par)


_INS = ["x_prompt", "x_sample", "cache_k", "cache_v", "state_pool", "norm_mix_g", "w_in", "b_gate", "lambda_q1",
        "lambda_k1", "lambda_q2", "lambda_k2", "subln_g", "pool_w", "pool_scale", "w_pool_branch", "w_attn_branch",
        "w_out", "norm_ffn_g", "w_router_group", "b_router_group", "w_router_expert", "b_router_expert",
        "w_expert_gate", "w_expert_up", "w_expert_down", "final_norm_g"]
_OUTS = [("y_prompt", (1, SEQ, D)), ("y_sample", (1, DEC, D)),
         ("new_k_prompt", (1, 1, SEQ, HEADS, P)), ("new_v_prompt", (1, 1, SEQ, HEADS, P)),
         ("new_pool_prompt", (1, 1, BUF, POOLW)),
         ("new_k_sample", (1, 1, DEC, HEADS, P)), ("new_v_sample", (1, 1, DEC, HEADS, P)),
         ("new_pool_sample", (1, 1, BUF, POOLW))]


def kernel(**inputs):
    import concourse.bacc as bacc
    from concourse.bass_utils import run_bass_kernel_spmd

    nc = bacc.Bacc("TRN2", target_bir_lowering=False, num_devices=1)
    arrays, a, o = {}, {}, {}
    for name in _INS:
        arrays[f"in_{name}"] = np.ascontiguousarray(inputs[name])
    arrays["in_cst"] = constants()
    for name in _INS + ["cst"]:
        v = arrays[f"in_{name}"]
        a[name] = nc.dram_tensor(f"in_{name}", v.shape, F32, kind="ExternalInput").ap()
    for name, shape in _OUTS:
        o[name] = nc.dram_tensor(f"out_{name}", shape, F32, kind="ExternalOutput").ap()
    build(nc, a, o)
    r = run_bass_kernel_spmd(nc, [arrays], core_ids=[0])
    return tuple(r.results[0][f"out_{name}"] for name, _ in _OUTS)
```

```python
import math
from contextlib import ExitStack

import concourse.bass as bass
import numpy as np
from concourse import mybir

F32 = mybir.dt.float32
F32R = mybir.dt.float32r
I32 = mybir.dt.int32
ALU = mybir.AluOpType
ACT = mybir.ActivationFunctionType
AX = mybir.AxisListType

P = 128
D = 1024
KD = D // P
SEQ, DEC, PAST = 512, 32, 128
TOK = SEQ + DEC
HALF = TOK // 2
NT = 5
LAST = P - DEC
HEADS, HD, CHUNK = 8, 64, 64
POOLW, NG, GD, BUF = 512, 4, 128, 15
WINDOWS = (2, 4, 8, 16)
EPS = 1e-6
SCALE = HD ** -0.5
LAM_INIT = 0.8 - 0.6 * math.exp(-0.3 * 0)
ROT, THETA = 16, 500000.0
EXPERTS, EG, EPG, HID = 16, 4, 4, 512
Q0, GATE0 = POOLW, POOLW + 3 * D
NEG = -1e30
CLAMP, BIG_SCALE, BIG_SUM = 1.5e18, 2.0 ** -70, 2.0 ** 116
TILES_PER_EXPERT = -(-TOK // P)
ROWS = TILES_PER_EXPERT * EXPERTS
NO_ROW = 2048
UW = BUF + SEQ + BUF + DEC
US = BUF + SEQ + BUF
SLOT = 1024
RA, S, RM = 4, 4, 24

C_ID, C_COS, C_SIN, C_INV, C_TRI, C_ONE = 0, 128, 288, 448, 508, 636
C_NEGH, C_NEGA, C_IOTA, C_VAL, C_LIST, C_STEP, C_TILE, C_NONE, C_EPS, C_SLOT, C_W = (
    764, 892, 1020, 1036, 1041, 1051, 1055, 1060, 1061, 1062, 1190)


def constants():
    c = np.zeros((P, C_W), np.float32)
    c[:, C_ID:C_ID + P] = np.eye(P)
    pos = np.arange(NT * P).reshape(NT, P)
    pos[4] = np.concatenate([np.arange(SEQ - LAST, SEQ), PAST + np.arange(DEC)])
    inv = np.power(np.float32(THETA), -np.arange(0, ROT, 2, dtype=np.float32) / np.float32(ROT)).astype(np.float32)
    ang = (pos.astype(np.float32)[..., None] * inv).astype(np.float32)
    for col, f in ((C_COS, np.cos), (C_SIN, np.sin)):
        t = np.broadcast_to(f(ang)[:, :, None, :], (NT, P, 4, ROT // 2)).transpose(1, 0, 2, 3)
        c[:, col:col + 160] = t.reshape(P, 160)
    for g, w in enumerate(WINDOWS):
        c[:, C_INV + BUF * g:C_INV + BUF * (g + 1)] = 1.0 / np.minimum(w, np.arange(BUF) + 1)
    c[:, C_TRI:C_TRI + P] = np.triu(np.ones((P, P)), 1)
    c[:, C_ONE:C_ONE + P] = 1.0
    c[:, C_NEGH:C_NEGH + CHUNK] = NEG
    c[:, C_NEGA:C_NEGA + P] = NEG
    c[:, C_IOTA:C_IOTA + EXPERTS] = np.arange(EXPERTS) - 99
    valid = np.ones((P, NT))
    valid[:LAST, 4] = 0
    c[:, C_VAL:C_VAL + NT] = valid
    tok = np.arange(NT * P).reshape(NT, P).T.astype(np.float32)
    tok[:, 4] = np.arange(SEQ - LAST, TOK)
    for k in range(2):
        c[:, C_LIST + NT * k:C_LIST + NT * (k + 1)] = valid * (2 * tok + k + 1)
    c[:, C_STEP:C_STEP + TILES_PER_EXPERT - 1] = P * np.arange(1, TILES_PER_EXPERT)
    c[:, C_TILE:C_TILE + TILES_PER_EXPERT] = np.arange(TILES_PER_EXPERT)
    c[:, C_NONE] = NO_ROW + 1 + np.arange(P)
    c[:, C_EPS] = EPS
    c[:, C_SLOT:C_SLOT + P] = np.arange(P)
    return c


def build(nc, a, o):
    base0 = nc.sbuf_base
    base0 = (base0 + 63) // 64 * 64
    K = 1024
    ends = [0]

    def at(name, off, shape, dt=F32):
        n = int(np.prod(shape[1:])) * 4
        ends[0] = max(ends[0], off + n)
        return nc.alloc_sbuf_tensor_at(name, shape, dt, offset=base0 + off)

    def region(off):
        pos = [off]

        def take(name, shape, dt=F32):
            t = at(name, pos[0], shape, dt)
            pos[0] += (int(np.prod(shape[1:])) * 4 + 31) // 32 * 32
            return t
        take.pos = pos
        return take

    with ExitStack() as ctx:
        sem = lambda n: ctx.enter_context(nc.semaphore(n))

        wh = at("wh", 0, [P, S, SLOT], F32R)
        wl = at("wl", 16 * K, [P, S, SLOT], F32R)
        x = at("x", 32 * K, [P, NT, D])
        small = region(52 * K)
        cst = small("cst", [P, C_W])
        bg = small("bg", [P, 16])
        psc = small("psc", [P, NG])
        sbg = small("sbg", [P, 1])
        lamv = small("lamv", [P, 4, HD])
        lame = small("lame", [P, 2])
        nlam = small("nlam", [P, 1])
        rsx = small("rsx", [P, NT])
        mx = small("mx", [P, 2, 2])
        nb = small("nb", [P, 2, 2])
        esum = small("esum", [P, 2, 2])
        rinv = small("rinv", [P, 2, 2])
        ssa = small("ssa", [P, NT, HEADS])
        rsa = small("rsa", [P, NT, HEADS])
        ssb = small("ssb", [P, NT, HEADS])
        isb = small("isb", [P, NT, HEADS])
        fin = small("fin", [P, NT, HEADS])
        wgt = small("wgt", [P, NT, 2])
        idi = small("idi", [P, ROWS + 2], I32)
        ydi = small("ydi", [P, ROWS], I32)
        wr = small("wr", [P, KD, EG + EXPERTS])
        rb = small("rb", [P, EG + EXPERTS])
        idn = small("idn", [P, 2], I32)
        ydn = small("ydn", [P, 2], I32)
        over = small("over", [P, 1], I32)
        assert small.pos[0] <= 60 * K + 384, small.pos[0]
        HR = 60 * K + 384
        hr = region(HR)
        qkv = hr("qkv", [P, NT, 384])
        E = hr("E", [P, 2, 2, 512])
        Am = hr("Am", [P, 512])
        qkh = hr("qkh", [P, 2, TOK], F32R)
        qkl = hr("qkl", [P, 2, TOK], F32R)
        ckh = hr("ckh", [P, P], F32R)
        ckl = hr("ckl", [P, P], F32R)
        vh = hr("vh", [P, NT + 1, P], F32R)
        vl = hr("vl", [P, NT + 1, P], F32R)
        ckv = hr("ckv", [P, 2, P])
        ath = hr("ath", [P, 4, P], F32R)
        atl = hr("atl", [P, 4, P], F32R)
        assert hr.pos[0] <= 99 * K, hr.pos[0]
        r0 = region(HR)
        sq = r0("sq", [P, 2, D])
        xn = r0("xn", [P, 2, D])
        r1 = region(HR)
        dd = r1("dd", [P, NG, TOK])
        ddh = r1("ddh", [P, NG, TOK], F32R)
        ddl = r1("ddl", [P, NG, TOK], F32R)
        B1 = r1("B1", [P, NG, UW])
        r2 = region(HR)
        mh = r2("mh", [P, KD, TOK], F32R)
        ml = r2("ml", [P, KD, TOK], F32R)
        rsq = at("rsq", r2.pos[0], [P, D])
        gt = r2("gt", [P, 2, TOK])
        assert r2.pos[0] <= 99 * K
        r3 = region(HR)
        xg = r3("xg", [P, 2, D])
        xh = r3("xh", [P, KD, P], F32R)
        xl = r3("xl", [P, KD, P], F32R)
        slot_hot = at("slot_hot", r3.pos[0], [P, 2, NT, P], F32R)
        hid = r3("hid", [P, HID])
        hsl = r3("hsl", [P, HID])
        hh = r3("hh", [P, 4, P], F32R)
        hl = r3("hl", [P, 4, P], F32R)
        yb = r3("yb", [P, 2, D])
        oht = r3("oht", [P, 2, NT, EXPERTS])
        assert r3.pos[0] <= 99 * K, r3.pos[0]
        att = at("att", 99 * K, [P, NT, HEADS, P])
        r4 = region(100 * K + 512)
        plh = r4("plh", [P, NG, TOK], F32R)
        pll = r4("pll", [P, NG, TOK], F32R)
        hTh = at("hTh", 119 * K, [P, KD, TOK], F32R)
        hTl = at("hTl", 136 * K, [P, KD, TOK], F32R)
        mA = at("mA", 153 * K, [P, KD, TOK])
        U = at("U", 153 * K, [P, NG, UW])
        B2 = at("B2", 162 * K, [P, NG - 1, UW])
        gate = at("gate", 170 * K, [P, KD, TOK])
        rawA = at("rawA", 187 * K, [P, RA, SLOT])
        rawM = at("rawM", 99 * K, [P, RM, SLOT])
        r5 = region(195 * K)
        h2T = r5("h2T", [P, KD, P])
        lg = r5("lg", [P, NT, EG + EXPERTS])
        ra = [r5(f"ra{i}", [P, NT, EXPERTS]) for i in range(4)]
        chosen = r5("chosen", [P, 2, NT, EXPERTS])
        cum = r5("cum", [P, NT + 1, EXPERTS])
        pk = r5("pk", [P, 2, NT])
        pj = r5("pj", [P, 2, NT])
        ge = r5("ge", [P, 2, NT, TILES_PER_EXPERT])
        lv = r5("lv", [P, ROWS])
        lw = r5("lw", [P, ROWS])
        rt = r5("rt", [P, 16, NT])
        assert r5.pos[0] <= 203 * K, r5.pos[0]
        woh = [at(f"woh{i}", o * K, [P, 2, SLOT], F32R) for i, o in enumerate((99, 119))]
        wol = [at(f"wol{i}", o * K, [P, 2, SLOT], F32R) for i, o in enumerate((107, 127))]
        hb = at("hb", 187 * K, [P, 2, D])
        item_hot = at("item_hot", 195 * K, [P, 2, NT, TILES_PER_EXPERT, EXPERTS], F32R)
        fy = at("fy", 99 * K, [P, NT, 2, D])
        ob = at("ob", 139 * K, [P, NT, D])
        fsq = at("fsq", 159 * K, [P, 2, D])
        gb = at("gb", 203 * K, [P, D])
        rot = at("rot", 203 * K, [P, 4, 160])
        asq = at("asq", 203 * K + 2560, [P, 2, P])
        bsq = at("bsq", 203 * K + 3584, [P, P])
        stt = at("stt", 116 * K, [16, POOLW])
        pst = at("pst", 203 * K, [P, 2, POOLW])
        assert ends[0] + base0 <= nc.sbuf_usable_end, (ends[0], base0, nc.sbuf_usable_end)

        ps = ctx.enter_context(nc.psum_tensor("ps", [P, 8, 512], F32))

        h2d = nc.dram_tensor("h2_rows", [TOK, D], F32, kind="Internal").ap()
        yd = nc.dram_tensor("expert_rows", [2 * TOK, D], F32, kind="Internal").ap()

        cst_in, w_small, x_in = sem("cst_in"), sem("w_small"), [sem(f"x_in{t}") for t in range(NT)]
        raw_in = [sem(f"raw_in{i}") for i in range(RA)]
        raw_h = [sem(f"raw_head{i}") for i in range(RA)]
        hi_done, lo_done, mm_done = sem("hi_done"), sem("lo_done"), sem("mm_done")
        dch, ach = sem("dve_chain"), sem("act_chain")
        ms_done, rt_done, xn_done, xt_mm, xt_hi, xt_lo = (sem(n) for n in (
            "ms_done", "root_done", "xn_done", "xt_mm", "xt_hi", "xt_lo"))
        st_in, st_mm, st_ev, pad_done = sem("state_in"), sem("state_mm"), sem("state_ev"), sem("pad_done")
        last_mm, ws_act, ws_dve, pool_done, dh_done, dl_done = (sem(n) for n in (
            "last_mm", "ws_act", "ws_dve", "pool_done", "pool_hi", "pool_lo"))
        out_done, lam_s, lam_e, lam_done = sem("out_done"), sem("lam_sums"), sem("lam_exp"), sem("lam_done")
        acc_mm, acc_ev, rope_done, vhi_done, vlo_done, ckv_in, kv_out = (sem(n) for n in (
            "acc_mm", "acc_ev", "rope_done", "vhi_done", "vlo_done", "ckv_in", "kv_out"))
        tr_mm, tr_hi, tr_lo, sc_mm, nb_done, exp_done, am_done, ta_mm, ath_done, atl_done, av_mm, av_ev = (
            sem(n) for n in ("tr_mm", "tr_hi", "tr_lo", "sc_mm", "nb_done", "exp_done", "am_done", "ta_mm",
                             "ath_done", "atl_done", "av_mm", "av_ev"))
        an_done, at_mm, at_hi, at_lo = sem("an_done"), sem("at_mm"), sem("at_hi"), sem("at_lo")
        ab_sum, ab_hi, ab_lo, o_mm, o_ev = (sem(n) for n in (
            "ab_sum", "ab_hi", "ab_lo", "o_mm", "o_ev"))
        gb_in, h2_done, h2_mm, h2_ev, lg_mm, gd_done, ge_done, sel_done, pos_mm, hot_done, ls_mm, id_done, xg_clear = (
            sem(n) for n in ("gain_in", "h2_done", "h2_mm", "h2_ev", "lg_mm", "gd_done", "ge_done",
                             "sel_done", "pos_mm", "hot_done", "list_mm", "id_done", "xg_clear"))
        cum_done, gb_mm, gb_ev, gate_done = sem("cum_done"), sem("gate_mm"), sem("gate_ev"), sem("gate_done")
        sp_go = sem("sp_go")
        m_raw = [sem(f"m_raw{i}") for i in range(RM)]
        m_hi, m_lo, m_mm, p_ch, p_go, xg_mm, xg_hi, xg_lo = (sem(n) for n in (
            "m_hi", "m_lo", "m_mm", "pool_chain", "pool_go", "xg_mm", "xg_hi", "xg_lo"))
        si_done, hid_done, hid_mm, hid_hi, hid_lo, y_ev = (sem(n) for n in (
            "silu_done", "hid_done", "hid_mm", "hid_hi", "hid_lo", "y_ev"))
        g_in = [sem(f"gather_in{i}") for i in range(2)]
        y_out = [sem(f"y_out{i}") for i in range(2)]
        Y0 = (3 * 16, 2 * 16)
        fy_in = [sem(f"fy_in{i}") for i in range(NT)]
        f_out, f_sum, f_rt, f_done = (sem(n) for n in ("f_out", "f_sum", "f_root", "f_done"))
        s_sum, s_rt, s_done, s_ch = (sem(n) for n in ("sample_sum", "sample_root", "sample_done", "sample_chain"))
        s_inv = sem("sample_inverse")

        id_m = cst[:, C_ID:C_ID + P]
        col = lambda t: slice(P * t, P * t + P) if t < 4 else slice(TOK - P, TOK)
        w_in = a["w_in"][0]

        def columns(w, c0, rows0, rows=4):
            return w[rows0 * P:(rows0 + rows) * P, c0:c0 + 256].rearrange("(k p) n -> p k n", p=P)

        ws, jobs = [], []

        def job(stage, i, views):
            jobs.append((stage, i, list(range(len(ws), len(ws) + len(views)))))
            ws.extend(views)
        for i in range(2):
            job("u", i, [columns(w_in, 256 * i, 4 * q) for q in range(2)])
        for i in range(4):
            job("gA", i, [columns(w_in, GATE0 + 256 * i, 4 * q) for q in range(2)])
        jobs.append(("last", 0, []))
        job("pl", 0, [a["pool_w"][0].rearrange("g c e -> c g e")])
        jobs.append(("pl", 1, [len(ws) - 1]))
        for i in range(4):
            job("pA", i, [columns(a["w_pool_branch"][0], 256 * i, 0)])
        H0 = len(ws)
        GB0 = H0 + 4 * HEADS
        AB0 = GB0 + 8
        O0 = AB0 + 8
        NCH = O0 + 8
        act_jobs = [j for j, (s, _, _) in enumerate(jobs) if s != "pA"]
        dve_jobs = [j for j, (s, _, _) in enumerate(jobs) if s in ("pl", "pA")]
        count = lambda js, j: sum(1 for v in js if v <= j)
        WH = 768
        GATE_BLOCKS = {0: (2,), 2: (3,), 3: (4,), 4: (5,)}

        def words(n):
            if n < H0:
                return 512 if n == jobs[7][2][0] else SLOT
            return WH if n < GB0 else SLOT

        def later_source(n):
            if n < AB0:
                m, q = divmod(n - GB0, 2)
                return columns(w_in, GATE0 + D + 256 * m, 4 * q)
            if n < O0:
                m, q = divmod(n - AB0, 2)
                return columns(a["w_attn_branch"][0], 256 * m, 4 * q)
            m, q = divmod(n - O0, 4)
            return a["w_out"][0][2 * P * q:2 * P * (q + 1), 512 * m:512 * (m + 1)].rearrange("(k p) n -> p k n", p=P)

        def head_source(h, k):
            return w_in[P * k:P * (k + 1), Q0:Q0 + 3 * D].rearrange(
                "p (s h c) -> p s h c", s=3, h=HEADS)[:, :, h, :]

        def arrival(n):
            return raw_in[n % RA], 16 * sum(1 for m in range(n + 1) if m % RA == n % RA and not H0 <= m < GB0)

        def raw_view(n, src):
            d = rawA[:, n % RA, 0:words(n)]
            return d.rearrange("p (k n) -> p k n", k=src.shape[1])

        new_k, new_v = o["new_k_prompt"][0, 0], o["new_v_prompt"][0, 0]
        new_ks, new_vs = o["new_k_sample"][0, 0], o["new_v_sample"][0, 0]
        moe_src = (a["w_expert_gate"][0], a["w_expert_up"][0], a["w_expert_down"][0])

        def split_slot(n):
            if n < O0 + S:
                return wh[:, n % S, :], wl[:, n % S, :]
            i, j = divmod(n - O0 - S, 2)
            return woh[i][:, j, :], wol[i][:, j, :]

        block = ctx.enter_context(nc.Block())

        @block.sync
        def _(sp):
            xp, xs = a["x_prompt"][0], a["x_sample"][0]
            sp.dma_start(x[:, 0, :], xp[0:P]).then_inc(x_in[0], 16)
            sp.dma_start(gb[:], a["norm_mix_g"][0].partition_broadcast(P)).then_inc(gb_in, 16)
            sp.dma_start(cst[:], a["cst"]).then_inc(cst_in, 16)

            def load(n, src):
                if n >= RA:
                    sp.wait_ge(lo_done, n - RA + 1)
                sp.dma_start(raw_view(n, src), src).then_inc(raw_in[n % RA], 16)
            for t in range(1, 4):
                sp.dma_start(x[:, t, :], xp[t * P:(t + 1) * P]).then_inc(x_in[t], 16)
            sp.dma_start(x[0:LAST, 4, :], xp[SEQ - LAST:SEQ]).then_inc(x_in[4], 16)
            sp.dma_start(x[LAST:P, 4, :], xs).then_inc(x_in[4], 16)
            for n in range(4):
                load(n, ws[n])
            sp.dma_start(stt[0:BUF, :], a["state_pool"][0, 0]).then_inc(st_in, 16)
            sp.dma_start(bg[:], a["b_gate"][0].rearrange("(c p) -> p c", p=P), allow_slow_non_contiguous=True).then_inc(w_small, 16)
            sp.dma_start(psc[:], a["pool_scale"][0].rearrange("(c p) -> p c", p=P), allow_slow_non_contiguous=True).then_inc(w_small, 16)
            sp.dma_start(sbg[:], a["subln_g"][0].rearrange("(p c) -> p c", c=1)).then_inc(w_small, 16)
            for i, n in enumerate(("lambda_q1", "lambda_k1", "lambda_q2", "lambda_k2")):
                sp.dma_start(lamv[:, i, :], a[n][0].partition_broadcast(P)).then_inc(w_small, 16)
            sp.dma_start(wr[:, :, 0:EG], a["w_router_group"][0].rearrange("(k p) g -> p k g", p=P)).then_inc(w_small, 16)
            for g in range(EG):
                sp.dma_start(wr[:, :, EG + EPG * g:EG + EPG * (g + 1)],
                             a["w_router_expert"][0, g].rearrange("(k p) e -> p k e", p=P)).then_inc(w_small, 16)
            sp.dma_start(rb[:, 0:EG], a["b_router_group"][0].partition_broadcast(P)).then_inc(w_small, 16)
            sp.dma_start(rb[:, EG:20], a["b_router_expert"][0].rearrange("g e -> (g e)").partition_broadcast(P)).then_inc(w_small, 16)
            for n in range(4, H0):
                load(n, ws[n])
                if n == H0 - 1:
                    sp.wait_ge(ws_act, count(act_jobs, 6))
                    for k, dst in enumerate((o["new_pool_prompt"], o["new_pool_sample"])):
                        sp.dma_start(dst[0, 0], pst[P - BUF:P, k, :]).then_inc(out_done, 16)
            def load_head(n, h, q):
                sp.wait_ge(lo_done, n - RA + 1)
                sp.sem_inc(sp_go, 1)
                for k in range(2):
                    d = rawA[:, (H0 + q) % RA, 384 * k:384 * k + 384].rearrange("p (s c) -> p s c", s=3)
                    sp.dma_start(d, head_source(h, 2 * q + k)).then_inc(raw_h[(H0 + q) % RA], 16)
            for q in range(4):
                load_head(H0 + q, 0, q)
            sp.wait_ge(ws_dve, len(dve_jobs))
            for k in range(2):
                sp.dma_start(ckv[:, k, :], a[("cache_k", "cache_v")[k]][0, 0, :, 0, :]).then_inc(ckv_in, 16)

            def head_loads(h):
                g = h - 1
                for q in range(4):
                    n = H0 + 4 * h + 4 + q
                    if isinstance(h, int) and h == HEADS - 1:
                        load(n, later_source(n))
                    else:
                        load_head(n, h + 1, q)
                    if q == 0:
                        head_out(g)
                        sp.wait_ge(tr_mm, 2 * g + 2)
                        sp.wait_ge(vlo_done, g + 1)
                        sp.sem_inc(sp_go, 1)
                        for k in range(2):
                            sp.dma_start(ckv[:, k, :], a[("cache_k", "cache_v")[k]][0, 0, :, g + 1, :]).then_inc(ckv_in, 16)

            def head_out(g):
                sp.wait_ge(rope_done, g + 1)
                sp.sem_inc(sp_go, 1)
                for j, (dp, ds) in enumerate(((new_k, new_ks), (new_v, new_vs))):
                    c = slice(P * (j + 1), P * (j + 2))
                    sp.dma_start(dp[:, g, :].rearrange("(t p) c -> p t c", p=P), qkv[:, 0:4, c]).then_inc(kv_out, 16)
                    sp.dma_start(ds[:, g, :], qkv[LAST:P, 4, c]).then_inc(kv_out, 16)

            for q in range(4):
                load_head(H0 + 4 + q, 1, q)
            with sp.Fori(1, HEADS - 1) as h:
                head_loads(h)
            head_loads(HEADS - 1)
            head_out(HEADS - 1)
            sp.wait_ge(ws_act, len(act_jobs))
            for n in range(GB0 + 4, O0):
                src = later_source(n)
                load(n, src)
            sp.wait_ge(an_done, 1)
            sp.dma_start(gb[:], a["norm_ffn_g"][0].partition_broadcast(P)).then_inc(gb_in, 16)

            def moe_load(slot, e, c):
                d = rawM[:, slot, :]
                if c < 8:
                    half, q = divmod(c, 4)
                    d = d.rearrange("p (k m n) -> p k m n", k=2, m=2)
                    for m in range(2):
                        src = moe_src[m][e, 2 * P * q:2 * P * (q + 1), 256 * half:256 * (half + 1)]
                        sp.dma_start(d[:, :, m, :], src.rearrange("(k p) n -> p k n", p=P)).then_inc(m_raw[slot], 16)
                else:
                    sp.dma_start(d, moe_src[2][e, P * (c - 8):P * (c - 7), :]).then_inc(m_raw[slot], 16)

            for n in range(O0, NCH):
                load(n, later_source(n))
            sp.wait_ge(ab_lo, 4)
            early = [4] + list(range(9, RM - 2))
            for s in early:
                moe_load(s, s // 12, s % 12)
            sp.wait_ge(o_mm, NT)
            for s in range(9):
                if s not in early:
                    moe_load(s, s // 12, s % 12)
            sp.wait_ge(h2_done, NT)
            sp.dma_start(gb[:], a["final_norm_g"].partition_broadcast(P)).then_inc(gb_in, 16)
            for par in range(2):
                sp.wait_ge(y_out[par], Y0[par])
            sp.wait_ge(h2_mm, NT)
            for s in (RM - 2, RM - 1):
                moe_load(s, 1, s % 12)

            def next_load(slot, e, c, n):
                sp.wait_ge(m_lo, n - RM + 1)
                sp.sem_inc(sp_go, 1)
                moe_load(slot, e, c)

            with sp.Fori(0, EXPERTS // 2 - 1) as ip:
                for par in range(2):
                    for c in range(12):
                        next_load(12 * par + c, 2 * ip + 2 + par, c, 24 * ip + 24 + 12 * par + c)
            for c in range(3):
                next_load(c, 0, c, 12 * EXPERTS + c)
            sp.wait_ge(id_done, 1)
            more = sp.value_load(over[0:1, 0:1], min_val=0, max_val=1)
            with sp.If(more > 0):
                with sp.Fori(1, TILES_PER_EXPERT) as j:
                    with sp.Fori(0, EXPERTS // 2) as eh:
                        for par in range(2):
                            for c in range(3 if par == 0 else 0, 12):
                                next_load(12 * par + c, 2 * eh + par, c, 192 * j + 24 * eh + 12 * par + c)
                        nxt = sp.snap((2 * eh + 2) % EXPERTS)
                        for c in range(3):
                            next_load(c, nxt, c, 192 * j + 24 * eh + 24 + c)
                for par in range(2):
                    sp.wait_ge(y_out[par], Y0[par] + 8 * ROWS)
                sp.wait_ge(m_lo, 12 * ROWS + 3)
                for c in range(3):
                    sp.wait_ge(m_raw[c], 32 * (ROWS // 2 + 1))
            for par in range(2):
                sp.wait_ge(y_out[par], Y0[par] + 8 * EXPERTS)
            sp.wait_ge(m_lo, 12 * EXPERTS + 3)
            pairs = yd.rearrange("(t k) d -> t k d", k=2)
            for t in range(4):
                sp.dma_start(fy[:, t], pairs[P * t:P * (t + 1)]).then_inc(fy_in[t], 16)
                if t == 0:
                    sp.dma_start(fy[LAST:P, 4], pairs[SEQ:TOK]).then_inc(fy_in[4], 16)
            for t in range(4):
                sp.wait_ge(f_done, t + 1)
                sp.dma_start(o["y_prompt"][0, t * P:(t + 1) * P], ob[:, t, :]).then_inc(f_out, 16)
                if t == 2:
                    sp.wait_ge(s_done, 1)
                    sp.dma_start(o["y_sample"][0], ob[LAST:P, 4, :]).then_inc(f_out, 16)
            sp.wait_ge(f_out, 16 * NT)
            sp.wait_ge(kv_out, 64 * HEADS)
            for c in range(3):
                sp.wait_ge(m_raw[c], 32 * (EXPERTS // 2 + 1))

        @block.gpsimd
        def _(pool):
            def gather(i, par, copies):
                pool.tensor_copy(idn[:, par:par + 1], idi[:, bass.ds(i, 1)]).then_inc(p_ch, 1)
                pool.wait_ge(p_ch, copies)
                pool.sem_inc(p_go, 1)
                pool.indirect_dma_start(xg[:, par, :], None, h2d[:, :],
                                        bass.IndirectOffsetOnAxis(ap=idn[:, par:par + 1], axis=0),
                                        bounds_check=TOK - 1, oob_is_err=False).then_inc(g_in[par], 16)

            def scatter(i, par):
                pool.wait_ge(y_ev, 2 * i + 3)
                pool.sem_inc(p_go, 1)
                pool.tensor_copy(ydn[:, par:par + 1], ydi[:, bass.ds(i, 1)]).then_inc(p_ch, 1)
                pool.wait_ge(p_ch, 2 * i + 4)
                pool.sem_inc(p_go, 1)
                pool.indirect_dma_start(yd[:, :], bass.IndirectOffsetOnAxis(ap=ydn[:, par:par + 1], axis=0),
                                        yb[:, par, :], None, bounds_check=2 * TOK - 1, oob_is_err=False).then_inc(y_out[par], 16)
            for t in range(NT):
                pool.wait_ge(h2_done, t + 1)
                if t < 4:
                    pool.dma_start(h2d[t * P:(t + 1) * P], hb[:, t % 2, :]).then_inc(y_out[t % 2], 16)
                else:
                    pool.dma_start(h2d[SEQ:TOK], hb[LAST:P, t % 2, :]).then_inc(y_out[t % 2], 16)
            pool.wait_ge(o_mm, NT)
            pool.memset(xg[:], 0.0).then_inc(xg_clear, 1)
            pool.wait_ge(xg_clear, 1)
            for par in range(2):
                pool.wait_ge(y_out[par], Y0[par])
            pool.wait_ge(id_done, 1)
            gather(0, 0, 1)
            gather(1, 1, 2)

            def pair(ip):
                for par in range(2):
                    i = 2 * ip + par
                    pool.wait_ge(xg_mm, i + 1)
                    pool.sem_inc(p_go, 1)
                    gather(i + 2, par, 2 * i + 3)
                    scatter(i, par)
            with pool.Fori(0, EXPERTS // 2) as ip:
                pair(ip)
            more = pool.value_load(over[0:1, 0:1], min_val=0, max_val=1)
            with pool.If(more > 0):
                with pool.Fori(EXPERTS // 2, ROWS // 2) as ip:
                    pair(ip)

            r, xt = slice(LAST, P), x[LAST:P, 4, :]
            pool.wait_ge(gb_in, 48)
            pool.wait_ge(fy_in[4], 16)
            for k in range(2):
                nc.gpsimd.tensor_scalar(fy[r, 4, k, :], fy[r, 4, k, :], wgt[r, 4, k:k + 1], None, ALU.mult).then_inc(s_ch, 1)
                pool.wait_ge(s_ch, 2 * k + 1)
                ins = nc.gpsimd.tensor_tensor(xt, fy[r, 4, k, :], xt, ALU.add)
                if k == 0:
                    ins.then_inc(s_ch, 1)
                    pool.wait_ge(s_ch, 2)
            ins.then_inc(s_sum, 1)
            pool.wait_ge(s_inv, 1)
            nc.gpsimd.tensor_scalar(ob[r, 4, :], xt, rsx[r, 4:5], None, ALU.mult).then_inc(s_ch, 1)
            pool.wait_ge(s_ch, 4)
            nc.gpsimd.tensor_tensor(ob[r, 4, :], ob[r, 4, :], gb[r], ALU.mult).then_inc(s_done, 1)

        @block.scalar
        def _(act):
            def hi(n, w=None):
                if H0 <= n < GB0:
                    act.wait_ge(raw_h[n % RA], 32 * ((n - H0) // 4 + 1))
                else:
                    act.wait_ge(*arrival(n))
                if n >= O0 + S:
                    act.wait_ge(at_mm, NT)
                    if n >= O0 + S + 2:
                        act.wait_ge(mm_done, O0)
                elif n >= S:
                    act.wait_ge(mm_done, n - S + 1)
                w = words(n)
                nc.scalar.activation(split_slot(n)[0][:, 0:w], rawA[:, n % RA, 0:w], ACT.Copy).then_inc(hi_done, 1)

            split = [0]

            def split_to(n):
                while split[0] <= n:
                    hi(split[0])
                    split[0] += 1

            def root(rows, t, scratch, done):
                roots[0] += 1
                nc.scalar.activation(scratch, x[rows, t, :], ACT.Square, accum_out=rsx[rows, t:t + 1]).then_inc(ach, 1)
                act.wait_ge(ach, roots[0])
                nc.scalar.activation(rsx[rows, t:t + 1], rsx[rows, t:t + 1], ACT.Sqrt, scale=1.0 / D,
                                     bias=cst[rows, C_EPS:C_EPS + 1]).then_inc(done, 1)
            roots, every = [0], slice(0, P)

            for t in range(NT):
                act.wait_ge(x_in[t], 16 if t < 4 else 32)
                if t == 0:
                    act.wait_ge(cst_in, 16)
                root(every, t, sq[:, t % 2, :], rt_done)
            for t in range(NT):
                act.wait_ge(xt_mm, t + 1)
                b, n0, c0 = 2 * (t % 4), P if t < 4 else DEC, P * t
                v = ps[:, b:b + 2, :].rearrange("p b (k n) -> p b k n", k=4)[:, :, :, P - n0:P]
                nc.scalar.activation(hTh[:, :, c0:c0 + n0].rearrange("p (b k) n -> p b k n", b=2), v,
                                     ACT.Copy).then_inc(xt_hi, 1)
                split_to(t - 1)
            act.wait_ge(st_mm, 1)
            act.wait_ge(pad_done, 1)
            nc.scalar.activation(U[:, :, BUF + SEQ:US], ps[:, 2, :].rearrange("p (g n) -> p g n", g=4)[:, :, 0:BUF],
                                 ACT.Copy).then_inc(st_ev, 1)
            act.wait_ge(lam_s, 1)
            nc.scalar.activation(lame[:], lame[:], ACT.Exp).then_inc(lam_e, 1)
            act.wait_ge(w_small, 14 * 16)
            for j, (stage, i, chunks) in enumerate(jobs):
                if chunks:
                    split_to(min(chunks[-1] + 3, H0 + 2))
                b = 4 * (j % 2)
                acc = ps[:, b:b + 4, 0:HALF].rearrange("p (c h) n -> p c h n", c=2)
                if stage == "pA":
                    continue
                if stage == "last":
                    act.wait_ge(last_mm, 1)
                else:
                    act.wait_ge(mm_done, chunks[-1] + 1)
                if stage == "u":
                    n1 = SEQ - HALF
                    nc.scalar.activation(U[:, 2 * i:2 * i + 2, BUF:BUF + HALF], acc[:, :, 0, :], ACT.Copy)
                    nc.scalar.activation(U[:, 2 * i:2 * i + 2, BUF + HALF:BUF + SEQ], acc[:, :, 1, 0:n1], ACT.Copy)
                    nc.scalar.activation(U[:, 2 * i:2 * i + 2, US:UW], acc[:, :, 1, n1:HALF], ACT.Copy).then_inc(ws_act, 1)
                elif stage == "gA":
                    for c in range(2):
                        ins = nc.scalar.activation(gate[:, 2 * i + c, :].rearrange("p (h n) -> p h n", h=2), acc[:, c],
                                                   ACT.Sigmoid, bias=bg[:, 2 * i + c:2 * i + c + 1])
                    ins.then_inc(ws_act, 1)
                    if i == 2:
                        act.wait_ge(pool_done, 1)
                        nc.scalar.activation(ddh[:], dd[:], ACT.Copy).then_inc(dh_done, 1)
                elif stage == "last":
                    nc.scalar.activation(pst[96:P, :, :], ps[96:P, b:b + 2, :], ACT.Copy).then_inc(ws_act, 1)
                elif stage == "pl":
                    for c in range(2):
                        g = 2 * i + c
                        ins = nc.scalar.activation(plh[:, g, :].rearrange("p (h n) -> p h n", h=2), acc[:, c],
                                                   ACT.Copy, scale=psc[:, g:g + 1])
                    ins.then_inc(ws_act, 1)

            def hi_head(q, n, rnd, w=WH):
                sl = (H0 + q) % S
                if w == WH:
                    act.wait_ge(raw_h[sl], 32 * (rnd + 1))
                else:
                    act.wait_ge(*arrival(n))
                act.wait_ge(mm_done, n - S + 1)
                nc.scalar.activation(wh[:, sl, 0:w], rawA[:, sl, 0:w], ACT.Copy).then_inc(hi_done, 1)

            def evacuate(h):
                for t in range(NT):
                    if t < 4:
                        act.wait_ge(acc_mm, 4 * h + t + 1)
                    else:
                        act.wait_ge(mm_done, H0 + 4 * h + 4)
                    if t == 0 and not (isinstance(h, int) and h == 0):
                        act.wait_ge(kv_out, 64 * h)
                        act.wait_ge(tr_lo, 3 * h)
                        act.wait_ge(vlo_done, h)
                    nc.scalar.activation(qkv[:, t, :], ps[:, t, 0:384], ACT.Copy).then_inc(acc_ev, 1)

            def step(g, s):
                if s >= 2:
                    act.wait_ge(av_mm, NT * g + s - 1)
                    nc.scalar.activation(bsq[:], ps[:, 7, 0:P], ACT.Square, scale=BIG_SCALE,
                                         accum_out=ssb[:, s - 2, bass.ds(g, 1)])
                    nc.scalar.activation(att[:, s - 2, g, :], ps[:, 7, 0:P], ACT.Copy).then_inc(av_ev, 1)
                if 1 <= s <= NT:
                    kb = s if s < NT else 2
                    act.wait_ge(ta_mm, NT * g + s)
                    nc.scalar.activation(ath[:, 0:kb, :], ps[:, 7, 0:kb * P].rearrange("p (k n) -> p k n", k=kb),
                                         ACT.Copy).then_inc(ath_done, 1)
                if s < NT:
                    n = P * (s + 1) if s < 4 else 2 * P
                    act.wait_ge(nb_done, NT * g + s + 1)
                    if s >= 2:
                        act.wait_ge(am_done, NT * g + s - 1)
                    elif not (isinstance(g, int) and g == 0):
                        act.wait_ge(am_done, NT * g)
                    for m in range(2):
                        ins = nc.scalar.activation(E[:, s % 2, m, 0:n], ps[:, 5 + m, 0:n], ACT.Exp,
                                                   bias=nb[:, s % 2, m:m + 1], scale=SCALE,
                                                   accum_out=esum[:, s % 2, m:m + 1])
                    ins.then_inc(exp_done, 1)

            def attend(g, nxt, gate_blocks={}):
                act.wait_ge(acc_ev, NT * (g + 1))
                if not (isinstance(g, int) and g == 0):
                    act.wait_ge(av_mm, NT * g)
                act.wait_ge(ckv_in, 32 * (g + 1))
                nc.scalar.activation(vh[:, 0:NT, :], qkv[:, :, 2 * P:3 * P], ACT.Copy)
                nc.scalar.activation(vh[:, NT, :], ckv[:, 1, :], ACT.Copy).then_inc(vhi_done, 1)
                nxt(3)
                act.wait_ge(tr_mm, 2 * g + 1)
                nc.scalar.activation(qkh[:, :, 0:SEQ], ps[:, 5:7, :], ACT.Copy).then_inc(tr_hi, 1)
                act.wait_ge(tr_mm, 2 * g + 2)
                v = ps[:, 7, 0:2 * P].rearrange("p (m n) -> p m n", m=2)
                nc.scalar.activation(qkh[:, :, SEQ:TOK], v[:, :, LAST:P], ACT.Copy).then_inc(tr_hi, 1)
                nc.scalar.activation(ckh[:], ps[:, 7, 2 * P:3 * P], ACT.Copy).then_inc(tr_hi, 1)
                nxt(4)
                for s in range(NT):
                    for b in gate_blocks.get(s, ()):
                        gate_block(b)
                    step(g, s)
                    if s == 2:
                        nxt(5)
                    if s == 4:
                        nxt(6)

            def gate_block(b):
                if b % 2:
                    act.wait_ge(mm_done, GB0 + b + 1)
                else:
                    act.wait_ge(gb_mm, b // 2 + 1)
                nc.scalar.activation(gate[:, b, :].rearrange("p (h n) -> p h n", h=2),
                                     ps[:, 2 * (b % 2):2 * (b % 2) + 2, 0:HALF], ACT.Copy).then_inc(gb_ev, 1)

            split_to(H0 + 6)
            act.wait_ge(out_done, 32)
            evacuate(0)

            def head(h, w_next=WH):
                n = H0 + 4 * h
                if not (isinstance(h, int) and h == 1):
                    step(h - 2, NT)
                    step(h - 2, NT + 1)
                attend(h - 1, lambda k: hi_head(k % 4, n + k, h + k // 4, WH if k == 3 else w_next))
                evacuate(h)
            head(1)
            with act.Fori(2, HEADS - 1) as h:
                head(h)
            head(HEADS - 1, SLOT)
            act.wait_ge(ws_dve, len(dve_jobs))
            split[0] = GB0 + 3
            gate_block(0)
            step(HEADS - 2, NT)
            gate_block(1)
            step(HEADS - 2, NT + 1)
            attend(HEADS - 1, lambda k: split_to({3: GB0 + 3, 4: GB0 + 5, 5: GB0 + 7, 6: AB0 + 1}[k]), GATE_BLOCKS)
            gate_block(6)
            step(HEADS - 1, NT)
            step(HEADS - 1, NT + 1)

            act.wait_ge(ms_done, 1)
            nc.scalar.activation(rsa[:], rsa[:], ACT.Sqrt).then_inc(rt_done, 1)
            gate_block(7)
            for t in range(NT):
                act.wait_ge(at_mm, t + 1)
                b, n0, c0 = 2 * (t % 4), P if t < 4 else DEC, P * t
                v = ps[:, b:b + 2, :].rearrange("p b (k n) -> p b k n", k=4)[:, :, :, P - n0:P]
                nc.scalar.activation(hTh[:, :, c0:c0 + n0].rearrange("p (b k) n -> p b k n", b=2), v,
                                     ACT.Copy, scale=sbg[:, 0:1]).then_inc(at_hi, 1)
            split_to(AB0 + 3)
            for c in range(KD):
                if c == 0:
                    act.wait_ge(gb_ev, KD)
                nc.scalar.activation(gate[:, c, :], gate[:, c, :], ACT.Sigmoid, bias=bg[:, KD + c:KD + c + 1]).then_inc(gate_done, 1)
            for m in range(4):
                split_to(AB0 + 2 * m + 4)
                act.wait_ge(ab_sum, m + 1)
                nc.scalar.activation(mh[:, 2 * m:2 * m + 2, :], mA[:, 2 * m:2 * m + 2, :], ACT.Copy).then_inc(ab_hi, 1)
            split_to(NCH - 1)
            for t in range(NT):
                act.wait_ge(o_ev, t + 1)
                root(every, t, rsq[:], rt_done)
                act.wait_ge(h2_mm, t + 1)
                if t:
                    act.wait_ge(lg_mm, t)
                else:
                    act.wait_ge(lo_done, NCH)
                nc.scalar.activation(h2T[:].rearrange("p (b k) n -> p b k n", b=2),
                                     ps[:, 4:6, :].rearrange("p b (k n) -> p b k n", k=4), ACT.Copy).then_inc(h2_ev, 1)
            act.wait_ge(gd_done, 1)
            nc.scalar.activation(rt[:, 8:13, :], rt[:, 8:13, :], ACT.Exp).then_inc(ge_done, 1)

            def m_hi_split(n, par, c, rnd, first=False):
                slot = 12 * par + c
                act.wait_ge(m_raw[slot], (32 if c < 8 else 16) * (rnd + 1))
                if first:
                    act.wait_ge(o_mm, NT)
                else:
                    act.wait_ge(m_mm, n - S + 2)
                nc.scalar.activation(wh[:, c % S, :], rawM[:, slot, :], ACT.Copy).then_inc(m_hi, 1)

            def rows_hi(i, par):
                act.wait_ge(xg_mm, i + 1)
                nc.scalar.activation(xh[:].rearrange("p (b k) n -> p b k n", b=2),
                                     ps[:, 2:4, :].rearrange("p b (k n) -> p b k n", k=4), ACT.Copy).then_inc(xg_hi, 1)

            def item(ip, par):
                i = 2 * ip + par
                n0 = 24 * ip + 12 * par

                def ahead(c):
                    if c < 12:
                        m_hi_split(n0 + c, par, c, ip)
                    else:
                        m_hi_split(n0 + c, 1 - par, c - 12, ip + par)
                for c in range(3, 7):
                    ahead(c)
                for half in range(2):
                    act.wait_ge(m_mm, n0 + 4 * half + 5)
                    act.wait_ge(hid_done, 2 * i + half + 1)
                    nc.scalar.activation(hsl[:, 256 * half:256 * half + 256], ps[:, half, 0:256], ACT.Silu).then_inc(si_done, 1)
                    if half == 0:
                        ahead(7)
                        act.wait_ge(hid_mm, 2 * i + 1)
                        nc.scalar.activation(hh[:, 0:2, :], ps[:, 4, 0:256].rearrange("p (k n) -> p k n", k=2),
                                             ACT.Copy).then_inc(hid_hi, 1)
                        for c in range(8, 11):
                            ahead(c)
                ahead(11)
                act.wait_ge(hid_mm, 2 * i + 2)
                nc.scalar.activation(hh[:, 2:4, :], ps[:, 4, 256:512].rearrange("p (k n) -> p k n", k=2),
                                     ACT.Copy).then_inc(hid_hi, 1)
                rows_hi(i + 1, 1 - par)
                for c in range(12, 15):
                    ahead(c)
                act.wait_ge(m_mm, n0 + 13)
                act.wait_ge(y_out[par], Y0[par] + 16 * ip)
                for b in range(2):
                    nc.scalar.activation(yb[:, par, 512 * b:512 * b + 512], ps[:, 5 + b, :], ACT.Copy).then_inc(y_ev, 1)
            for c in range(3):
                m_hi_split(c, 0, c, 0, first=True)
            act.sem_inc(y_ev, 1)
            rows_hi(0, 0)
            with act.Fori(0, EXPERTS // 2) as ip:
                for par in range(2):
                    item(ip, par)
            act.wait_ge(id_done, 1)
            more = act.value_load(over[0:1, 0:1], min_val=0, max_val=1)
            with act.If(more > 0):
                with act.Fori(EXPERTS // 2, ROWS // 2) as ip:
                    for par in range(2):
                        item(ip, par)
            for t in range(4):
                act.wait_ge(f_sum, t + 1)
                root(every, t, fsq[:, t % 2, :], f_rt)
                if t == 2:
                    act.wait_ge(s_sum, 1)
                    root(slice(LAST, P), 4, fsq[LAST:P, 1, :], s_rt)

        @block.vector
        def _(dve):
            V = nc.vector
            links = [0]

            def link(ins, base=0):
                links[0] += 1
                ins.then_inc(dch, 1)
                dve.wait_ge(dch, base + links[0])

            def lo(n):
                dve.wait_ge(hi_done, n + 1)
                w = words(n)
                h, l = split_slot(n)
                V.tensor_tensor(l[:, 0:w], rawA[:, n % RA, 0:w], h[:, 0:w].bitcast(F32),
                                ALU.subtract).then_inc(lo_done, 1)

            split = [0]

            def split_to(n):
                while split[0] <= n:
                    lo(split[0])
                    split[0] += 1

            V.memset(U[:, :, 0:BUF], 0.0).then_inc(pad_done, 1)
            V.memset(idi[:, ROWS:ROWS + 2], 0)
            dve.wait_ge(gb_in, 16)

            def rows_lo(t):
                b, n0, c0 = 2 * (t % 4), P if t < 4 else DEC, P * t
                v = ps[:, b:b + 2, :].rearrange("p b (k n) -> p b k n", k=4)[:, :, :, P - n0:P]
                oh = hTh[:, :, c0:c0 + n0].bitcast(F32).rearrange("p (b k) n -> p b k n", b=2)
                ol = hTl[:, :, c0:c0 + n0].rearrange("p (b k) n -> p b k n", b=2)
                return v, oh, ol

            for t in range(NT + 1):
                if t < NT:
                    dve.wait_ge(rt_done, t + 1)
                    link(V.reciprocal(rsx[:, t:t + 1], rsx[:, t:t + 1]))
                    if t >= 2:
                        dve.wait_ge(xt_mm, t - 1)
                    V.scalar_tensor_tensor(out=xn[:, t % 2, :], in0=x[:, t, :], scalar=rsx[:, t:t + 1], in1=gb[:],
                                           op0=ALU.mult, op1=ALU.mult).then_inc(xn_done, 1)
                if t:
                    dve.wait_ge(xt_hi, t)
                    v, oh, ol = rows_lo(t - 1)
                    V.tensor_tensor(ol, v, oh, ALU.subtract).then_inc(xt_lo, 1)
                    split_to(t - 2)
            dve.wait_ge(w_small, 14 * 16)
            for i in range(2):
                ins = V.scalar_tensor_tensor(out=lamv[:, 2 * i, :], in0=lamv[:, 2 * i, :], scalar=1.0,
                                             in1=lamv[:, 2 * i + 1, :], op0=ALU.mult, op1=ALU.mult,
                                             accum_out=lame[:, i:i + 1])
            ins.then_inc(lam_s, 1)
            V.tensor_scalar(sbg[:], sbg[:], 1.0 - LAM_INIT, None, ALU.mult)
            dve.wait_ge(lam_e, 1)
            V.scalar_tensor_tensor(out=nlam[:], in0=lame[:, 1:2], scalar=-LAM_INIT, in1=lame[:, 0:1],
                                   op0=ALU.add, op1=ALU.subtract).then_inc(lam_done, 1)

            def pool_steps():
                dve.wait_ge(ws_act, 2)
                dve.wait_ge(st_ev, 1)
                link(V.tensor_tensor(B1[:, :, 1:UW], U[:, :, 1:UW], U[:, :, 0:UW - 1], ALU.add))
                yield
                link(V.tensor_tensor(B2[:, :, 3:UW], B1[:, 1:4, 3:UW], B1[:, 1:4, 1:UW - 2], ALU.add))
                yield
                link(V.tensor_tensor(B1[:, 2:4, 7:UW], B2[:, 1:3, 7:UW], B2[:, 1:3, 3:UW - 4], ALU.add))
                yield
                link(V.tensor_tensor(B2[:, 2, 15:UW], B1[:, 3, 15:UW], B1[:, 3, 7:UW - 8], ALU.add))
                for g, w in enumerate(WINDOWS):
                    sums = B1[:, g, :] if g % 2 == 0 else B2[:, g - 1, :]
                    inv = cst[:, C_INV + BUF * g:C_INV + BUF * (g + 1)]
                    V.tensor_tensor(dd[:, g, 0:BUF], sums[:, BUF:2 * BUF], inv, ALU.mult)
                    V.scalar_tensor_tensor(out=dd[:, g, BUF:SEQ], in0=sums[:, 2 * BUF:BUF + SEQ], scalar=1.0 / w,
                                           in1=U[:, g, 2 * BUF:BUF + SEQ], op0=ALU.mult, op1=ALU.subtract)
                    link(V.scalar_tensor_tensor(out=dd[:, g, SEQ:TOK], in0=sums[:, US:UW], scalar=1.0 / w,
                                                in1=U[:, g, US:UW], op0=ALU.mult, op1=ALU.subtract))
                    ins = V.tensor_tensor(dd[:, g, 0:BUF], dd[:, g, 0:BUF], U[:, g, BUF:2 * BUF], ALU.subtract)
                    if g == NG - 1:
                        ins.then_inc(pool_done, 1)
                    yield

            steps = pool_steps()
            split_to(6)
            for j, (stage, i, chunks) in enumerate(jobs):
                b = 4 * (j % 2)
                acc = ps[:, b:b + 4, 0:HALF].rearrange("p (c h) n -> p c h n", c=2)
                if chunks:
                    split_to(min(chunks[-1] + 3, H0 + 2))
                if stage == "gA":
                    for _ in range(4):
                        next(steps, None)
                if stage == "last":
                    dve.wait_ge(dh_done, 1)
                    V.tensor_tensor(ddl[:], dd[:], ddh[:].bitcast(F32), ALU.subtract).then_inc(dl_done, 1)
                if stage == "pl":
                    dve.wait_ge(ws_act, count(act_jobs, j))
                    for c in range(2):
                        g = 2 * i + c
                        ins = V.scalar_tensor_tensor(out=pll[:, g, :].rearrange("p (h n) -> p h n", h=2), in0=acc[:, c],
                                                     scalar=psc[:, g:g + 1],
                                                     in1=plh[:, g, :].bitcast(F32).rearrange("p (h n) -> p h n", h=2),
                                                     op0=ALU.mult, op1=ALU.subtract)
                    ins.then_inc(ws_dve, 1)
                if stage == "pA":
                    dve.wait_ge(ws_act, count(act_jobs, j))
                    dve.wait_ge(mm_done, chunks[-1] + 1)
                    V.tensor_tensor(mA[:, 2 * i:2 * i + 2, :].rearrange("p c (h n) -> p c h n", h=2), acc,
                                    gate[:, 2 * i:2 * i + 2, :].rearrange("p c (h n) -> p c h n", h=2),
                                    ALU.mult).then_inc(ws_dve, 1)

            def lo_head(q, n, w=WH):
                sl = (H0 + q) % S
                dve.wait_ge(hi_done, n + 1)
                V.tensor_tensor(wl[:, sl, 0:w], rawA[:, sl, 0:w], wh[:, sl, 0:w].bitcast(F32),
                                ALU.subtract).then_inc(lo_done, 1)

            per_head = 1 + 5 * NT
            per_tail = 6

            def step(g, s, lk):
                if 1 <= s <= NT:
                    t = s - 1
                    n = P * (t + 1) if t < 4 else 2 * P
                    dve.wait_ge(exp_done, NT * g + s)
                    lk(V.reciprocal(rinv[:, t % 2, :], esum[:, t % 2, :]))
                    V.tensor_tensor(rinv[:, t % 2, 1:2], rinv[:, t % 2, 1:2], nlam[:], ALU.mult)
                    lk(V.tensor_scalar(E[:, t % 2, 0, 0:n], E[:, t % 2, 0, 0:n], rinv[:, t % 2, 0:1], None, ALU.mult))
                    if t:
                        dve.wait_ge(ta_mm, NT * g + t)
                    V.scalar_tensor_tensor(out=Am[:, 0:n], in0=E[:, t % 2, 1, 0:n], scalar=rinv[:, t % 2, 1:2],
                                           in1=E[:, t % 2, 0, 0:n], op0=ALU.mult, op1=ALU.add).then_inc(am_done, 1)
                if s < NT:
                    n = P * (s + 1) if s < 4 else 2 * P
                    dve.wait_ge(sc_mm, NT * g + s + 1)
                    lk(V.tensor_reduce(mx[:, s % 2, :], ps[:, 5:7, 0:n], AX.X, ALU.max))
                    V.tensor_scalar(nb[:, s % 2, :], mx[:, s % 2, :], -SCALE, None, ALU.mult).then_inc(nb_done, 1)
                if 1 <= s <= NT:
                    kb = s if s < NT else 2
                    dve.wait_ge(ath_done, NT * g + s)
                    V.tensor_tensor(atl[:, 0:kb, :], ps[:, 7, 0:kb * P].rearrange("p (k n) -> p k n", k=kb),
                                    ath[:, 0:kb, :].bitcast(F32), ALU.subtract).then_inc(atl_done, 1)
                if s >= 2:
                    dve.wait_ge(av_ev, NT * g + s - 1)
                    lk(V.tensor_scalar(asq[:, 0, :], att[:, s - 2, g, :], CLAMP, -CLAMP, ALU.min, ALU.max))
                    ins = V.scalar_tensor_tensor(out=asq[:, 1, :], in0=asq[:, 0, :], scalar=1.0,
                                                 in1=asq[:, 0, :], op0=ALU.mult, op1=ALU.mult,
                                                 accum_out=ssa[:, s - 2, bass.ds(g, 1)])
                    lk(ins)

            def rope(g, lk):
                v = qkv[:, :, 0:256].rearrange("p t (g d) -> p t g d", g=4)
                x1, x2 = v[:, :, :, 0:8], v[:, :, :, 8:16]
                cos = cst[:, C_COS:C_COS + 160].rearrange("p (t g d) -> p t g d", t=NT, g=4)
                sin = cst[:, C_SIN:C_SIN + 160].rearrange("p (t g d) -> p t g d", t=NT, g=4)
                tmp = [rot[:, r, :].rearrange("p (t g d) -> p t g d", t=NT, g=4) for r in range(4)]
                dve.wait_ge(acc_ev, NT * (g + 1))
                V.tensor_tensor(tmp[0], x1, cos, ALU.mult)
                V.tensor_tensor(tmp[1], x2, sin, ALU.mult)
                V.tensor_tensor(tmp[2], x2, cos, ALU.mult)
                lk(V.tensor_tensor(tmp[3], x1, sin, ALU.mult))
                V.tensor_tensor(x1, tmp[0], tmp[1], ALU.subtract)
                V.tensor_tensor(x2, tmp[2], tmp[3], ALU.add).then_inc(rope_done, 1)

            def attend(g, nxt, lk):
                dve.wait_ge(vhi_done, g + 1)
                V.tensor_tensor(vl[:, 0:NT, :], qkv[:, :, 2 * P:3 * P], vh[:, 0:NT, :].bitcast(F32), ALU.subtract)
                V.tensor_tensor(vl[:, NT, :], ckv[:, 1, :], vh[:, NT, :].bitcast(F32), ALU.subtract).then_inc(vlo_done, 1)
                nxt(3)
                dve.wait_ge(tr_hi, 3 * g + 1)
                V.tensor_tensor(qkl[:, :, 0:SEQ], ps[:, 5:7, :], qkh[:, :, 0:SEQ].bitcast(F32), ALU.subtract).then_inc(tr_lo, 1)
                dve.wait_ge(tr_hi, 3 * g + 3)
                w = ps[:, 7, 0:2 * P].rearrange("p (m n) -> p m n", m=2)
                V.tensor_tensor(qkl[:, :, SEQ:TOK], w[:, :, LAST:P], qkh[:, :, SEQ:TOK].bitcast(F32),
                                ALU.subtract).then_inc(tr_lo, 1)
                V.tensor_tensor(ckl[:], ps[:, 7, 2 * P:3 * P], ckh[:].bitcast(F32), ALU.subtract).then_inc(tr_lo, 1)
                nxt(4)
                for s in range(NT):
                    step(g, s, lk)
                    if s == 2:
                        nxt(5)
                    if s == 4:
                        nxt(6)

            dve.wait_ge(lam_done, 1)
            dve.wait_ge(out_done, 32)
            split_to(H0 + 6)
            d1 = links[0] + per_head - per_tail

            def head(h, w_next=WH):
                n = H0 + 4 * h
                first = isinstance(h, int) and h == 1
                base = 0 if first else d1 + per_head * (h - 2)
                if not first:
                    links[0] = 0
                lk = lambda ins: link(ins, base)
                rope(h - 1, lk)
                if not first:
                    step(h - 2, NT, lk)
                    step(h - 2, NT + 1, lk)
                attend(h - 1, lambda k: lo_head(k % 4, n + k, WH if k == 3 else w_next), lk)
                assert links[0] == (d1 if first else per_head)
            head(1)
            with dve.Fori(2, HEADS - 1) as h:
                head(h)
            head(HEADS - 1, SLOT)
            links[0] = d1 + per_head * (HEADS - 2)
            split[0] = GB0 + 3
            rope(HEADS - 1, link)
            step(HEADS - 2, NT, link)
            step(HEADS - 2, NT + 1, link)
            attend(HEADS - 1, lambda k: split_to({3: GB0 + 3, 4: GB0 + 5, 5: GB0 + 7, 6: AB0 + 1}[k]), link)
            step(HEADS - 1, NT, link)
            step(HEADS - 1, NT + 1, link)

            big, one = BIG_SUM / (BIG_SCALE ** -2), 2.0 ** 128 * BIG_SCALE ** 2
            link(V.tensor_scalar(fin[:], ssb[:], big, None, ALU.is_ge))
            link(V.tensor_scalar(isb[:], ssb[:], one, 2.0 ** -40 * BIG_SCALE ** -2 / P, ALU.min, ALU.mult))
            link(V.tensor_tensor(isb[:], isb[:], fin[:], ALU.mult))
            link(V.tensor_scalar(rsa[:], ssa[:], 2.0 ** -40 / P, 2.0 ** -40 * EPS, ALU.mult, ALU.add))
            link(V.tensor_scalar(fin[:], fin[:], -1.0, 1.0, ALU.mult, ALU.add))
            link(V.tensor_tensor(rsa[:], rsa[:], fin[:], ALU.mult))
            link(V.tensor_tensor(rsa[:], rsa[:], isb[:], ALU.add))
            V.tensor_scalar(fin[:], ssb[:], one, 2.0 ** -20, ALU.is_lt, ALU.mult).then_inc(ms_done, 1)
            dve.wait_ge(rt_done, NT + 1)
            link(V.reciprocal(rsa[:], rsa[:]))
            link(V.tensor_tensor(rsa[:], rsa[:], fin[:], ALU.mult))
            for t in range(NT + 1):
                if t < NT:
                    V.tensor_tensor(att[:, t], att[:, t], rsa[:, t, :].unsqueeze(2).broadcast_to([P, HEADS, P]),
                                    ALU.mult).then_inc(an_done, 1)
                if t:
                    dve.wait_ge(at_hi, t)
                    v, oh, ol = rows_lo(t - 1)
                    V.scalar_tensor_tensor(out=ol, in0=v, scalar=sbg[:, 0:1], in1=oh, op0=ALU.mult,
                                           op1=ALU.subtract).then_inc(at_lo, 1)
            for m in range(4):
                b = 4 * (m % 2)
                acc = ps[:, b:b + 4, 0:HALF].rearrange("p (c h) n -> p c h n", c=2)
                four = lambda r: r.rearrange("p c (h n) -> p c h n", h=2)
                split_to(AB0 + 2 * m + 4)
                dve.wait_ge(mm_done, AB0 + 2 * m + 2)
                dve.wait_ge(gate_done, 2 * m + 2)
                link(V.tensor_tensor(four(gt[:]), acc, four(gate[:, 2 * m:2 * m + 2, :]), ALU.mult))
                V.tensor_tensor(mA[:, 2 * m:2 * m + 2, :], mA[:, 2 * m:2 * m + 2, :], gt[:], ALU.add).then_inc(ab_sum, 1)
                dve.wait_ge(ab_hi, m + 1)
                V.tensor_tensor(ml[:, 2 * m:2 * m + 2, :], mA[:, 2 * m:2 * m + 2, :],
                                mh[:, 2 * m:2 * m + 2, :].bitcast(F32), ALU.subtract).then_inc(ab_lo, 1)
            split_to(NCH - 1)
            dve.wait_ge(gb_in, 32)
            for t in range(NT):
                dve.wait_ge(o_mm, t + 1)
                link(V.tensor_tensor(x[:, t, :].rearrange("p (b n) -> p b n", b=2), ps[:, 2 * (t % 2):2 * (t % 2) + 2, :],
                                     x[:, t, :].rearrange("p (b n) -> p b n", b=2), ALU.add))
                dve.sem_inc(o_ev, 1)
                dve.wait_ge(rt_done, NT + 2 + t)
                link(V.reciprocal(rsx[:, t:t + 1], rsx[:, t:t + 1]))
                if t >= 2:
                    dve.wait_ge(y_out[t % 2], 16 * (t // 2))
                    dve.wait_ge(h2_mm, t - 1)
                V.scalar_tensor_tensor(out=hb[:, t % 2, :], in0=x[:, t, :], scalar=rsx[:, t:t + 1], in1=gb[:],
                                       op0=ALU.mult, op1=ALU.mult).then_inc(h2_done, 1)
            V.memset(cum[:, 0, :], 0.0)
            dve.wait_ge(lg_mm, NT)
            bc = lambda r, n: r.unsqueeze(2).broadcast_to([P, NT, n])
            link(V.tensor_tensor(lg[:], ps[:, 6, 0:NT * 20].rearrange("p (t n) -> p t n", t=NT),
                                 rb[:].unsqueeze(1).broadcast_to([P, NT, 20]), ALU.add))
            iota = cst[:, C_IOTA:C_IOTA + EXPERTS].unsqueeze(1).broadcast_to([P, NT, EXPERTS])
            gl, el = lg[:, :, 0:EG], lg[:, :, EG:20]

            def first_max(src, n, m, onehot, scratch):
                link(V.tensor_reduce(m, src, AX.X, ALU.max))
                link(V.tensor_tensor(scratch, src, bc(m, n), ALU.is_equal))
                link(V.tensor_tensor(scratch, scratch, iota[:, :, 0:n], ALU.mult))
                link(V.tensor_reduce(rt[:, 15, :], scratch, AX.X, ALU.min))
                link(V.tensor_tensor(onehot, iota[:, :, 0:n], bc(rt[:, 15, :], n), ALU.is_equal))
            gmax, m1, m2 = rt[:, 0, :], rt[:, 1, :], rt[:, 2, :]
            first_max(gl, EG, gmax, ra[0][:, :, 0:EG], ra[1][:, :, 0:EG])
            link(V.tensor_scalar(ra[0][:, :, 0:EG], ra[0][:, :, 0:EG], -NEG, NEG, ALU.mult, ALU.add))
            link(V.tensor_tensor(ra[1][:].rearrange("p t (g e) -> p t g e", g=EG), el.rearrange("p t (g e) -> p t g e", g=EG),
                                 ra[0][:, :, 0:EG].unsqueeze(3).broadcast_to([P, NT, EG, EPG]), ALU.add))
            first_max(ra[1][:], EXPERTS, m1, chosen[:, 0], ra[3][:])
            link(V.scalar_tensor_tensor(out=ra[2][:], in0=chosen[:, 0], scalar=2 * NEG, in1=ra[1][:], op0=ALU.mult, op1=ALU.add))
            first_max(ra[2][:], EXPERTS, m2, chosen[:, 1], ra[3][:])
            link(V.tensor_tensor(ra[1][:], chosen[:, 0], chosen[:, 1], ALU.add))
            V.tensor_tensor(ra[1][:], ra[1][:], bc(cst[:, C_VAL:C_VAL + NT], EXPERTS), ALU.mult).then_inc(sel_done, 1)
            dve.wait_ge(sel_done, 1)
            link(V.tensor_copy(cum[:, 1, :], ra[1][:, 0, :]))
            for t in range(1, NT):
                ins = V.tensor_tensor(cum[:, t + 1, :], cum[:, t, :], ra[1][:, t, :], ALU.add)
                if t < NT - 1:
                    link(ins)
            ins.then_inc(cum_done, 1)
            V.tensor_tensor(rt[:, 8:12, :].rearrange("p g t -> p t g"), gl, bc(gmax, EG), ALU.subtract)
            V.tensor_tensor(rt[:, 12, :], m2, m1, ALU.subtract).then_inc(gd_done, 1)
            kt = lambda r, n: r.unsqueeze(3).broadcast_to([P, 2, NT, n])
            row = lambda c, n: cst[:, c:c + n].unsqueeze(1).unsqueeze(1).broadcast_to([P, 2, NT, n])
            values = cst[:, C_LIST:C_LIST + 2 * NT].rearrange("p (k t) -> p k t", k=2)
            link(V.tensor_tensor(oht[:], chosen[:], kt(values, EXPERTS), ALU.mult))
            dve.wait_ge(pos_mm, 1)
            pos = ps[:, 7, 0:NT * EXPERTS].rearrange("p (t e) -> p t e", t=NT).unsqueeze(1).broadcast_to([P, 2, NT, EXPERTS])
            link(V.tensor_tensor(chosen[:], chosen[:], pos, ALU.mult))
            link(V.tensor_reduce(pk[:], chosen[:], AX.X, ALU.add))
            link(V.tensor_tensor(ge[:, :, :, 0:4], kt(pk[:], 4), row(C_STEP, 4), ALU.is_ge))
            link(V.tensor_reduce(pj[:], ge[:, :, :, 0:4], AX.X, ALU.add))
            link(V.scalar_tensor_tensor(out=pk[:], in0=pj[:], scalar=float(-P), in1=pk[:], op0=ALU.mult, op1=ALU.add))
            link(V.tensor_tensor(ge[:], kt(pj[:], TILES_PER_EXPERT), row(C_TILE, TILES_PER_EXPERT), ALU.is_equal))
            for k in range(2):
                V.tensor_tensor(item_hot[:, k], ge[:, k].unsqueeze(3).broadcast_to([P, NT, TILES_PER_EXPERT, EXPERTS]),
                                oht[:, k].unsqueeze(2).broadcast_to([P, NT, TILES_PER_EXPERT, EXPERTS]), ALU.mult)
            for k in range(2):
                ins = V.tensor_tensor(slot_hot[:, k], pk[:, k].unsqueeze(2).broadcast_to([P, NT, P]),
                                      cst[:, C_SLOT:C_SLOT + P].unsqueeze(1).broadcast_to([P, NT, P]), ALU.is_equal)
                ins.then_inc(hot_done, 1)
            link(V.tensor_reduce(rt[:, 7, 0:1], ps[:, 7, 80:96], AX.X, ALU.max))
            V.tensor_scalar(over[:], rt[:, 7, 0:1], float(P), None, ALU.is_gt)
            dve.wait_ge(ls_mm, 1)
            link(V.tensor_scalar(lv[:], ps[:, 4, 0:ROWS], 0.5, cst[:, C_NONE:C_NONE + 1], ALU.is_lt, ALU.mult))
            link(V.scalar_tensor_tensor(out=ydi[:], in0=ps[:, 4, 0:ROWS], scalar=-1.0, in1=lv[:], op0=ALU.add, op1=ALU.add))
            V.tensor_scalar(idi[:, 0:ROWS], ydi[:], 1, None, ALU.logical_shift_right).then_inc(id_done, 1)
            dve.wait_ge(ge_done, 1)
            link(V.tensor_reduce(rt[:, 3, :], rt[:, 8:12, :].rearrange("p g t -> p t g"), AX.X, ALU.add))
            link(V.tensor_scalar(rt[:, 4, :], rt[:, 12, :], 1.0, None, ALU.add))
            link(V.tensor_tensor(rt[:, 4, :], rt[:, 4, :], rt[:, 3, :], ALU.mult))
            link(V.reciprocal(rt[:, 4, :], rt[:, 4, :]))
            V.tensor_copy(wgt[:, :, 0], rt[:, 4, :])
            V.tensor_tensor(wgt[:, :, 1], rt[:, 4, :], rt[:, 12, :], ALU.mult)

            def item(ip, par):
                i = 2 * ip + par
                n0 = 24 * ip + 12 * par

                def ahead(c):
                    slot = (12 * par + c) % RM
                    dve.wait_ge(m_hi, n0 + c + 1)
                    V.tensor_tensor(wl[:, c % S, :], rawM[:, slot, :], wh[:, c % S, :].bitcast(F32),
                                    ALU.subtract).then_inc(m_lo, 1)
                for c in range(3, 7):
                    ahead(c)
                for half in range(2):
                    hs = slice(256 * half, 256 * half + 256)
                    kk = slice(2 * half, 2 * half + 2)
                    dve.wait_ge(si_done, 2 * i + half + 1)
                    V.tensor_tensor(hid[:, hs], ps[:, half, 256:512], hsl[:, hs], ALU.mult).then_inc(hid_done, 1)
                    ahead(7 if half == 0 else 11)
                    dve.wait_ge(hid_hi, 2 * i + half + 1)
                    V.tensor_tensor(hl[:, kk, :], ps[:, 4, hs].rearrange("p (k n) -> p k n", k=2),
                                    hh[:, kk, :].bitcast(F32), ALU.subtract).then_inc(hid_lo, 1)
                    if half == 0:
                        for c in range(8, 11):
                            ahead(c)
                rows(i + 1)
                for c in range(12, 15):
                    ahead(c)

            def rows(i):
                dve.wait_ge(xg_hi, i + 1)
                V.tensor_tensor(xl[:].rearrange("p (b k) n -> p b k n", b=2),
                                ps[:, 2:4, :].rearrange("p b (k n) -> p b k n", k=4),
                                xh[:].bitcast(F32).rearrange("p (b k) n -> p b k n", b=2), ALU.subtract).then_inc(xg_lo, 1)
            for c in range(3):
                dve.wait_ge(m_hi, c + 1)
                V.tensor_tensor(wl[:, c, :], rawM[:, c, :], wh[:, c, :].bitcast(F32), ALU.subtract).then_inc(m_lo, 1)
            dve.sem_inc(hid_done, 1)
            rows(0)
            with dve.Fori(0, EXPERTS // 2) as ip:
                for par in range(2):
                    item(ip, par)
            more = dve.value_load(over[0:1, 0:1], min_val=0, max_val=1)
            with dve.If(more > 0):
                with dve.Fori(EXPERTS // 2, ROWS // 2) as ip:
                    for par in range(2):
                        item(ip, par)

            dve.wait_ge(gb_in, 48)
            for t in range(5):
                if t < 4:
                    dve.wait_ge(fy_in[t], 16)
                    link(V.scalar_tensor_tensor(out=x[:, t, :], in0=fy[:, t, 0, :], scalar=wgt[:, t, 0:1], in1=x[:, t, :],
                                                op0=ALU.mult, op1=ALU.add))
                    V.scalar_tensor_tensor(out=x[:, t, :], in0=fy[:, t, 1, :], scalar=wgt[:, t, 1:2], in1=x[:, t, :],
                                           op0=ALU.mult, op1=ALU.add).then_inc(f_sum, 1)
                if t:
                    u = t - 1
                    dve.wait_ge(f_rt, u + 1)
                    link(V.reciprocal(rsx[:, u:u + 1], rsx[:, u:u + 1]))
                    V.scalar_tensor_tensor(out=ob[:, u, :], in0=x[:, u, :], scalar=rsx[:, u:u + 1], in1=gb[:],
                                           op0=ALU.mult, op1=ALU.mult).then_inc(f_done, 1)
                if t == 3:
                    dve.wait_ge(s_rt, 1)
                    V.reciprocal(rsx[LAST:P, 4:5], rsx[LAST:P, 4:5]).then_inc(s_inv, 1)

        @block.tensor
        def _(pe):
            T = nc.tensor

            def three(out, sh, sl, mh_, ml_, start, stop, **kw):
                T.matmul(out, sh, mh_, start=start, stop=False, **kw)
                T.matmul(out, sh, ml_, start=False, stop=False, **kw)
                return T.matmul(out, sl, mh_, start=False, stop=stop, **kw)

            pe.wait_ge(cst_in, 16)
            for t in range(NT):
                pe.wait_ge(xn_done, t + 1)
                if t >= 4:
                    pe.wait_ge(xt_lo, t - 3)
                for k in range(KD):
                    ins = T.transpose(ps[:, 2 * (t % 4) + k // 4, P * (k % 4):P * (k % 4 + 1)],
                                      xn[:, t % 2, P * k:P * k + P], id_m)
                ins.then_inc(xt_mm, 1)
            pe.wait_ge(st_in, 16)
            pe.wait_ge(xt_lo, 2)
            for g in range(NG):
                ins = T.transpose(ps[:, 2, P * g:P * g + BUF], stt[0:BUF, P * g:P * g + P], cst[0:BUF, C_ID:C_ID + BUF])
            ins.then_inc(st_mm, 1)
            pe.wait_ge(xt_lo, NT)
            pe.wait_ge(st_ev, 1)

            def stationary(chunk_ids, banks, rhs_h, rhs_l, k_first, k_last):
                k = k_first
                for n in chunk_ids:
                    pe.wait_ge(lo_done, n + 1)
                    sl = n % S
                    for kk in range(4):
                        for c in range(2):
                            wc = slice(256 * kk + P * c, 256 * kk + P * (c + 1))
                            for h in range(2):
                                tc = slice(HALF * h, HALF * (h + 1))
                                ins = three(ps[:, banks + 2 * c + h, 0:HALF], wh[:, sl, wc], wl[:, sl, wc],
                                            rhs_h[:, k, tc], rhs_l[:, k, tc], k == 0, k == k_last)
                        k += 1
                    ins.then_inc(mm_done, 1)
                return ins

            for j, (stage, i, chunks) in enumerate(jobs):
                b = 4 * (j % 2)
                if j >= 2:
                    pe.wait_ge(ws_act, count(act_jobs, j - 2))
                    if count(dve_jobs, j - 2):
                        pe.wait_ge(ws_dve, count(dve_jobs, j - 2))
                if stage == "pA" and i == 0:
                    pe.wait_ge(ws_act, count(act_jobs, j - 1))
                    pe.wait_ge(ws_dve, count(dve_jobs, j - 1))
                if stage in ("u", "gA"):
                    stationary(chunks, b, hTh, hTl, 0, KD - 1)
                elif stage == "pA":
                    stationary(chunks, b, plh, pll, 0, NG - 1)
                elif stage == "last":
                    for k, c1 in enumerate((BUF + SEQ, UW)):
                        for g in range(NG):
                            ins = T.transpose(ps[:, b + k, P * g:P * g + P], U[:, g, c1 - P:c1], id_m)
                    ins.then_inc(last_mm, 1)
                else:
                    pe.wait_ge(lo_done, chunks[0] + 1)
                    pe.wait_ge(dl_done, 1)
                    sl = chunks[0] % S
                    for c in range(2):
                        wc = slice(P * (2 * i + c), P * (2 * i + c + 1))
                        for h in range(2):
                            tc = slice(HALF * h, HALF * (h + 1))
                            ins = three(ps[:, b + 2 * c + h, 0:HALF], wh[:, sl, wc], wl[:, sl, wc],
                                        ddh[:, 2 * i + c, tc], ddl[:, 2 * i + c, tc], True, True)
                    if i == 1:
                        ins.then_inc(mm_done, 1)

            def project(h, j):
                n = H0 + 4 * h + j // 2
                sl, k = (H0 + j // 2) % S, j % 2
                if k == 0:
                    pe.wait_ge(lo_done, n + 1)
                wc = slice(384 * k, 384 * k + 384)
                for t in range(NT):
                    if j == 0:
                        if isinstance(h, int) and h == 0:
                            if t == 0:
                                pe.wait_ge(ws_act, len(act_jobs))
                                pe.wait_ge(ws_dve, len(dve_jobs))
                        else:
                            pe.wait_ge(acc_ev, NT * (h - 1) + t + 1)
                    ins = three(ps[:, t, 0:384], hTh[:, j, col(t)], hTl[:, j, col(t)], wh[:, sl, wc], wl[:, sl, wc],
                                j == 0, j == KD - 1)
                    if j == KD - 1 and t < 4:
                        ins.then_inc(acc_mm, 1)
                if k == 1:
                    ins.then_inc(mm_done, 1)

            def turn(g):
                pe.wait_ge(rope_done, g + 1)
                if not (isinstance(g, int) and g == 0):
                    pe.wait_ge(av_ev, NT * g)
                for m in range(2):
                    for t in range(4):
                        ins = T.transpose(ps[:, 5 + m, P * t:P * t + P], qkv[:, t, P * m:P * m + P], id_m)
                ins.then_inc(tr_mm, 1)
                for m in range(2):
                    T.transpose(ps[:, 7, P * m:P * m + P], qkv[:, 4, P * m:P * m + P], id_m)
                pe.wait_ge(ckv_in, 32 * (g + 1))
                T.transpose(ps[:, 7, 2 * P:3 * P], ckv[:, 0, :], id_m).then_inc(tr_mm, 1)

            def scores(g, t):
                if t == 0:
                    pe.wait_ge(tr_lo, 3 * (g + 1))
                else:
                    pe.wait_ge(exp_done, NT * g + t)
                for m in range(2):
                    r = slice(HD * m, HD * m + HD)
                    qh, ql, out = qkh[r, 0, col(t)], qkl[r, 0, col(t)], ps[:, 5 + m, :]
                    neg = C_NEGH if t < 4 else C_NEGA
                    if t < 4:
                        n = P * (t + 1)
                        keys, hidden, kw = (out[:, 0:n], qkh[r, 1, 0:n], qkl[r, 1, 0:n]), out[:, n - CHUNK:n], {}
                    else:
                        three(out[:, 0:P], qh, ql, ckh[r, :], ckl[r, :], True, True)
                        keys, hidden = (out[:, P:2 * P], qkh[r, 1, col(4)], qkl[r, 1, col(4)]), out[:, P:P + LAST]
                        kw = dict(skip_group_check=True)
                    width = CHUNK if t < 4 else LAST
                    T.matmul(keys[0], qh, keys[1], start=t < 4, stop=False, **kw)
                    T.matmul(hidden, cst[0:1, neg:neg + P], cst[0:1, C_ONE:C_ONE + width], start=False, stop=False, **kw)
                    T.matmul(keys[0], qh, keys[2], start=False, stop=False, **kw)
                    ins = T.matmul(keys[0], ql, keys[1], start=False, stop=True, **kw)
                ins.then_inc(sc_mm, 1)

            def turn_probs(g, t):
                pe.wait_ge(am_done, NT * g + t + 1)
                if t:
                    pe.wait_ge(av_ev, NT * g + t)
                for kb in range(t + 1 if t < 4 else 2):
                    ins = T.transpose(ps[:, 7, P * kb:P * kb + P], Am[:, P * kb:P * kb + P], id_m)
                ins.then_inc(ta_mm, 1)

            def values(g, t):
                pe.wait_ge(atl_done, NT * g + t + 1)
                vs = range(t + 1) if t < 4 else (NT, 4)
                for kb, v in enumerate(vs):
                    ins = three(ps[:, 7, 0:P], ath[:, kb, :], atl[:, kb, :], vh[:, v, :], vl[:, v, :],
                                kb == 0, kb == len(vs) - 1)
                ins.then_inc(av_mm, 1)

            def attend_step(g, s):
                if s >= 2:
                    values(g, s - 2)
                if s < NT:
                    scores(g, s)
                if 1 <= s <= NT:
                    turn_probs(g, s - 1)

            for j in range(KD):
                project(0, j)

            def head(h):
                for j in range(2):
                    project(h, j)
                    if not (isinstance(h, int) and h == 1):
                        attend_step(h - 2, NT + j)
                turn(h - 1)
                project(h, 2)
                for s in range(NT):
                    attend_step(h - 1, s)
                    project(h, s + 3)
            head(1)
            with pe.Fori(2, HEADS - 1) as h:
                head(h)
            head(HEADS - 1)

            def gate_block(b):
                if b < 2:
                    pe.wait_ge(acc_ev, NT * (HEADS - 1) + 2 * b + 2)
                else:
                    pe.wait_ge(gb_ev, b - 1)
                for k in range(KD):
                    n = GB0 + 2 * (b // 2) + k // 4
                    if k % 4 == 0:
                        pe.wait_ge(lo_done, n + 1)
                    c0 = 256 * (k % 4) + P * (b % 2)
                    for h in range(2):
                        tc = slice(HALF * h, HALF * (h + 1))
                        ins = three(ps[:, 2 * (b % 2) + h, 0:HALF], wh[:, n % S, c0:c0 + P], wl[:, n % S, c0:c0 + P],
                                    hTh[:, k, tc], hTl[:, k, tc], k == 0, k == KD - 1)
                    if b % 2 and k == 3:
                        ins.then_inc(mm_done, 1)
                ins.then_inc(mm_done if b % 2 else gb_mm, 1)

            gate_block(0)
            attend_step(HEADS - 2, NT)
            gate_block(1)
            attend_step(HEADS - 2, NT + 1)
            turn(HEADS - 1)
            for s in range(NT):
                for b in GATE_BLOCKS.get(s, ()):
                    gate_block(b)
                attend_step(HEADS - 1, s)
            gate_block(6)
            attend_step(HEADS - 1, NT)
            attend_step(HEADS - 1, NT + 1)
            gate_block(7)

            for t in range(NT):
                pe.wait_ge(an_done, t + 1)
                if t == 0:
                    pe.wait_ge(acc_ev, NT * HEADS)
                if t < 2:
                    pe.wait_ge(gb_ev, KD - 1 + t)
                if t == 2:
                    pe.wait_ge(exp_done, NT * HEADS)
                if t == 3:
                    pe.wait_ge(av_ev, NT * HEADS)
                if t == 4:
                    pe.wait_ge(at_lo, 1)
                for k in range(KD):
                    ins = T.transpose(ps[:, 2 * (t % 4) + k // 4, P * (k % 4):P * (k % 4 + 1)], att[:, t, k, :], id_m)
                ins.then_inc(at_mm, 1)
            pe.wait_ge(at_lo, NT)
            for m in range(4):
                if m >= 2:
                    pe.wait_ge(ab_lo, m - 1)
                stationary([AB0 + 2 * m, AB0 + 2 * m + 1], 4 * (m % 2), hTh, hTl, 0, KD - 1)

            def turn_rows(t):
                pe.wait_ge(h2_done, t + 1)
                if t:
                    pe.wait_ge(h2_ev, t)
                for k in range(KD):
                    ins = T.transpose(ps[:, 4 + k // 4, P * (k % 4):P * (k % 4 + 1)], hb[:, t % 2, P * k:P * k + P], id_m)
                ins.then_inc(h2_mm, 1)

            def logits(t):
                pe.wait_ge(h2_ev, t + 1)
                for k in range(KD):
                    ins = T.matmul(ps[:, 6, 20 * t:20 * t + 20], h2T[:, k, :], wr[:, k, :], start=(k == 0), stop=(k == KD - 1))
                ins.then_inc(lg_mm, 1)

            for t in range(NT):
                if t >= 2:
                    pe.wait_ge(o_ev, t - 1)
                    turn_rows(t - 2)
                for m in range(2):
                    for q in range(4):
                        n = O0 + 4 * m + q
                        if t == 0:
                            pe.wait_ge(lo_done, n + 1)
                            pe.wait_ge(ab_lo, max(3, q + 1))
                        h, l = split_slot(n)
                        for kk in range(2):
                            wc = slice(512 * kk, 512 * kk + 512)
                            ins = three(ps[:, 2 * (t % 2) + m, :], mh[:, 2 * q + kk, col(t)], ml[:, 2 * q + kk, col(t)],
                                        h[:, wc], l[:, wc], q == kk == 0, q == 3 and kk == 1)
                    if m == 0 and t >= 2:
                        logits(t - 2)
                ins.then_inc(o_mm, 1)
            for t in (NT - 2, NT - 1):
                turn_rows(t)
                logits(t)
            pe.wait_ge(sel_done, 1)
            ones, tri = cst[:, C_ONE:C_ONE + P], cst[:, C_TRI:C_TRI + P]
            T.matmul(ps[:, 7, 0:NT * EXPERTS], tri, ra[1][:].rearrange("p t e -> p (t e)"), start=True, stop=False,
                     skip_group_check=True)
            pe.wait_ge(cum_done, 1)
            T.matmul(ps[:, 7, 0:NT * EXPERTS], ones, cum[:, 0:NT, :].rearrange("p t e -> p (t e)"), start=False, stop=True,
                     skip_group_check=True)
            T.matmul(ps[:, 7, NT * EXPERTS:(NT + 1) * EXPERTS], ones, cum[:, NT, :], start=True, stop=True,
                     skip_group_check=True).then_inc(pos_mm, 1)
            for k in range(2):
                pe.wait_ge(hot_done, k + 1)
                for t in range(NT):
                    ins = T.matmul(ps[:, 4, 0:ROWS], slot_hot[:, k, t, :],
                                   item_hot[:, k, t].rearrange("p j e -> p (j e)"), start=(k == t == 0), stop=(k == 1 and t == NT - 1))
            ins.then_inc(ls_mm, 1)

            def gathered(ip, par, i):
                pe.wait_ge(g_in[par], 16 * (ip + 1))
                pe.wait_ge(xg_lo, i)
                for k in range(KD):
                    ins = T.transpose(ps[:, 2 + k // 4, P * (k % 4):P * (k % 4 + 1)], xg[:, par, P * k:P * k + P], id_m)
                ins.then_inc(xg_mm, 1)

            def item(ip, par):
                i = 2 * ip + par
                n0 = 24 * ip + 12 * par

                def up(c):
                    pe.wait_ge(m_lo, n0 + c + 1)
                    for kk in range(2):
                        k = 2 * (c % 4) + kk
                        wc = slice(512 * kk, 512 * kk + 512)
                        ins = three(ps[:, c // 4, :], xh[:, k, :], xl[:, k, :], wh[:, c % S, wc], wl[:, c % S, wc],
                                    k == 0, k == KD - 1)
                    ins.then_inc(m_mm, 1)

                def turn_hidden(half):
                    pe.wait_ge(hid_done, 2 * i + half + 2)
                    for k in range(2 * half, 2 * half + 2):
                        ins = T.transpose(ps[:, 4, P * k:P * k + P], hid[:, P * k:P * k + P], id_m)
                    ins.then_inc(hid_mm, 1)

                def down(k):
                    c = 8 + k
                    pe.wait_ge(m_lo, n0 + c + 1)
                    for b in range(2):
                        wc = slice(512 * b, 512 * b + 512)
                        ins = three(ps[:, 5 + b, :], hh[:, k, :], hl[:, k, :], wh[:, c % S, wc], wl[:, c % S, wc],
                                    k == 0, k == 3)
                    ins.then_inc(m_mm, 1)
                pe.wait_ge(xg_lo, i + 1)
                pe.wait_ge(hid_done, 2 * i + 1)
                for c in range(6):
                    up(c)
                turn_hidden(0)
                up(6)
                up(7)
                pe.wait_ge(hid_lo, 2 * i + 1)
                pe.wait_ge(y_ev, 2 * i + 1)
                down(0)
                turn_hidden(1)
                down(1)
                gathered(ip + par, 1 - par, i + 1)
                pe.wait_ge(hid_lo, 2 * i + 2)
                down(2)
                down(3)
            pe.sem_inc(m_mm, 1)
            gathered(0, 0, 0)
            with pe.Fori(0, EXPERTS // 2) as ip:
                for par in range(2):
                    item(ip, par)
            pe.wait_ge(id_done, 1)
            more = pe.value_load(over[0:1, 0:1], min_val=0, max_val=1)
            with pe.If(more > 0):
                with pe.Fori(EXPERTS // 2, ROWS // 2) as ip:
                    for par in range(2):
                        item(ip, par)


_INS = ["x_prompt", "x_sample", "cache_k", "cache_v", "state_pool", "norm_mix_g", "w_in", "b_gate", "lambda_q1",
        "lambda_k1", "lambda_q2", "lambda_k2", "subln_g", "pool_w", "pool_scale", "w_pool_branch", "w_attn_branch",
        "w_out", "norm_ffn_g", "w_router_group", "b_router_group", "w_router_expert", "b_router_expert",
        "w_expert_gate", "w_expert_up", "w_expert_down", "final_norm_g"]
_OUTS = [("y_prompt", (1, SEQ, D)), ("y_sample", (1, DEC, D)),
         ("new_k_prompt", (1, 1, SEQ, HEADS, P)), ("new_v_prompt", (1, 1, SEQ, HEADS, P)),
         ("new_pool_prompt", (1, 1, BUF, POOLW)),
         ("new_k_sample", (1, 1, DEC, HEADS, P)), ("new_v_sample", (1, 1, DEC, HEADS, P)),
         ("new_pool_sample", (1, 1, BUF, POOLW))]


def kernel(**inputs):
    import concourse.bacc as bacc
    from concourse.bass_utils import run_bass_kernel_spmd

    nc = bacc.Bacc("TRN2", target_bir_lowering=False, num_devices=1)
    arrays, a, o = {}, {}, {}
    for name in _INS:
        arrays[f"in_{name}"] = np.ascontiguousarray(inputs[name])
    arrays["in_cst"] = constants()
    for name in _INS + ["cst"]:
        v = arrays[f"in_{name}"]
        a[name] = nc.dram_tensor(f"in_{name}", v.shape, F32, kind="ExternalInput").ap()
    for name, shape in _OUTS:
        o[name] = nc.dram_tensor(f"out_{name}", shape, F32, kind="ExternalOutput").ap()
    build(nc, a, o)
    r = run_bass_kernel_spmd(nc, [arrays], core_ids=[0])
    return tuple(r.results[0][f"out_{name}"] for name, _ in _OUTS)
```
